# Optimizing a Trainium2 kernel written in Bass

```python
import math
import jax, jax.numpy as jnp
from jax import lax
import numpy as np

D_MODEL = 1024
BATCH = 1
SEQ = 512
DEPTH = 1

PLE_DIM = 256
MIX_WIDTH = D_MODEL
ATTN_WIDTH = MIX_WIDTH // 2
SGU_WIDTH = MIX_WIDTH - ATTN_WIDTH
HEAD_DIM = 64
N_ATTN_HEADS = ATTN_WIDTH // HEAD_DIM
N_SGU_GROUPS = 4
SGU_GROUP_DIM = SGU_WIDTH // N_SGU_GROUPS
SGU_CHUNK = 128
DILATION_PAIRS = ((128, 1), (512, 4), (2048, 16))
QBLK = 128
D_FF = ((8 * D_MODEL + 3 * 256 - 1) // (3 * 256)) * 256
PROJ_COLS = 3 * ATTN_WIDTH + 2 * SGU_WIDTH
EPS = 1e-6
NEG = -1e30


def rmsnorm(x, g):
    xf = x.astype(jnp.float32)
    y = xf * lax.rsqrt(jnp.mean(xf * xf, axis=-1, keepdims=True) + EPS)
    return (y * g.astype(jnp.float32)).astype(x.dtype)

def layernorm(x, g, b):
    xf = x.astype(jnp.float32)
    mu = jnp.mean(xf, axis=-1, keepdims=True)
    xc = xf - mu
    y = xc * lax.rsqrt(jnp.mean(xc * xc, axis=-1, keepdims=True) + EPS)
    return (y * g.astype(jnp.float32) + b.astype(jnp.float32)).astype(x.dtype)

def dilated_branch(q, k, v, slopes, window, dilation):
    B, H, S, hd = q.shape
    span = dilation * QBLK
    s_pad = -(-S // span) * span
    M = s_pad // dilation
    nb = M // QBLK
    n_steps = window // dilation
    pad = ((0, 0), (0, 0), (0, s_pad - S), (0, 0))

    def to_blocks(t):
        t = jnp.pad(t, pad).reshape(B, H, M, dilation, hd).transpose(0, 1, 3, 2, 4)
        return t.reshape(B, H, dilation, nb, QBLK, hd)

    def with_prev(t):
        prev = jnp.pad(t, ((0, 0), (0, 0), (0, 0), (1, 0), (0, 0), (0, 0)))[:, :, :, :-1]
        return jnp.concatenate([prev, t], axis=-2)

    qb = to_blocks(q)
    kc = with_prev(to_blocks(k))
    vc = with_prev(to_blocks(v))
    s = jnp.einsum('bhrnqc,bhrnkc->bhrnqk', qb, kc)

    qi = jnp.arange(QBLK)[:, None]
    ki = jnp.arange(2 * QBLK)[None, :]
    steps = QBLK + qi - ki
    blk = jnp.arange(nb)[:, None, None]
    valid = (steps >= 0) & (steps <= n_steps) & (blk * QBLK - QBLK + ki >= 0)
    dist = (jnp.clip(steps, 0, None) * dilation).astype(jnp.float32)
    bias = -slopes[:, None, None] * dist[None]
    s = s + bias[None, :, None, None]
    s = jnp.where(valid[None, None, None], s, NEG)
    mx = jnp.max(s, axis=-1, keepdims=True)
    e = jnp.exp(s - mx)
    den = jnp.sum(e, axis=-1)
    o = jnp.einsum('bhrnqk,bhrnkc->bhrnqc', e, vc) / den[..., None]
    lse = mx[..., 0] + jnp.log(den)
    o = o.reshape(B, H, dilation, M, hd).transpose(0, 1, 3, 2, 4).reshape(B, H, s_pad, hd)[:, :, :S]
    lse = lse.reshape(B, H, dilation, M).transpose(0, 1, 3, 2).reshape(B, H, s_pad)[:, :, :S]
    return o, lse

def dilated_attention(q, k, v):
    B, S, _ = q.shape
    dtype = q.dtype

    def heads(t):
        return t.reshape(B, S, N_ATTN_HEADS, HEAD_DIM).transpose(0, 2, 1, 3).astype(jnp.float32)

    qh = heads(q) * (HEAD_DIM ** -0.5)
    kh, vh = heads(k), heads(v)
    slopes = 2.0 ** (-8.0 * (jnp.arange(N_ATTN_HEADS, dtype=jnp.float32) + 1.0) / N_ATTN_HEADS)
    outs, lses = [], []
    for window, dilation in DILATION_PAIRS:
        o, l = dilated_branch(qh, kh, vh, slopes, window, dilation)
        outs.append(o)
        lses.append(l)
    w = jax.nn.softmax(jnp.stack(lses, axis=0), axis=0)
    out = jnp.sum(w[..., None] * jnp.stack(outs, axis=0), axis=0)
    return out.transpose(0, 2, 1, 3).reshape(B, S, ATTN_WIDTH).astype(dtype)

def spatial_gating(u, z, ln_g, ln_b, w_s, b_s):
    B, S, _ = u.shape
    nc = S // SGU_CHUNK
    u = jax.nn.gelu(u).reshape(B, S, N_SGU_GROUPS, SGU_GROUP_DIM)
    z = jax.nn.gelu(z).reshape(B, S, N_SGU_GROUPS, SGU_GROUP_DIM)
    z = layernorm(z, ln_g, ln_b)
    zc = z.reshape(B, nc, SGU_CHUNK, N_SGU_GROUPS, SGU_GROUP_DIM)
    causal = jnp.tril(jnp.ones((SGU_CHUNK, SGU_CHUNK), dtype=w_s.dtype))
    wm = w_s * causal[None]
    mixed = jnp.einsum('gij,bnjgc->bnigc', wm, zc) + b_s.T[None, None, :, :, None]
    out = u * mixed.reshape(B, S, N_SGU_GROUPS, SGU_GROUP_DIM)
    return out.reshape(B, S, SGU_WIDTH)

def first_inputs(seed: int = 0) -> dict:
    key = jax.random.key(seed)
    ks = jax.random.split(key, 20)
    f32 = jnp.float32

    def nrm(k, shape, scale):
        return jax.random.normal(k, shape, f32) * scale

    def gain(k, shape):
        return 1.0 + 0.05 * jax.random.normal(k, shape, f32)

    L = DEPTH
    return {
        "x": jax.random.normal(ks[0], (BATCH, SEQ, D_MODEL), f32),
        "p": jax.random.normal(ks[1], (DEPTH, BATCH, SEQ, PLE_DIM), f32),
        "ln_pre_mix": gain(ks[2], (L, D_MODEL)),
        "w_in": nrm(ks[3], (L, D_MODEL, PROJ_COLS), D_MODEL ** -0.5),
        "sgu_ln_g": gain(ks[4], (L, SGU_GROUP_DIM)),
        "sgu_ln_b": nrm(ks[5], (L, SGU_GROUP_DIM), 0.02),
        "w_spatial": nrm(ks[6], (L, N_SGU_GROUPS, SGU_CHUNK, SGU_CHUNK), SGU_CHUNK ** -0.5),
        "b_spatial": gain(ks[7], (L, N_SGU_GROUPS, SGU_CHUNK)),
        "attn_out_norm": gain(ks[8], (L, ATTN_WIDTH)),
        "sgu_out_norm": gain(ks[9], (L, SGU_WIDTH)),
        "w_out": nrm(ks[10], (L, MIX_WIDTH, D_MODEL), MIX_WIDTH ** -0.5),
        "ln_post_mix": gain(ks[11], (L, D_MODEL)),
        "ln_pre_ffn": gain(ks[12], (L, D_MODEL)),
        "w_gate_up": nrm(ks[13], (L, D_MODEL, 2 * D_FF), D_MODEL ** -0.5),
        "w_down": nrm(ks[14], (L, D_FF, D_MODEL), D_FF ** -0.5),
        "ln_post_ffn": gain(ks[15], (L, D_MODEL)),
        "w_pe_gate": nrm(ks[16], (L, D_MODEL, D_MODEL), D_MODEL ** -0.5),
        "b_pe_gate": nrm(ks[17], (L, D_MODEL), 0.02),
        "w_pe_proj": nrm(ks[18], (L, PLE_DIM, D_MODEL), PLE_DIM ** -0.5),
    }

def first_block(x, p, ln_pre_mix, w_in, sgu_ln_g, sgu_ln_b, w_spatial, b_spatial,
              attn_out_norm, sgu_out_norm, w_out, ln_post_mix, ln_pre_ffn, w_gate_up,
              w_down, ln_post_ffn, w_pe_gate, b_pe_gate, w_pe_proj):
    h = x
    splits = [ATTN_WIDTH, 2 * ATTN_WIDTH, 3 * ATTN_WIDTH, 3 * ATTN_WIDTH + SGU_WIDTH]
    for i in range(DEPTH):
        a = rmsnorm(h, ln_pre_mix[i])
        proj = a @ w_in[i]
        q, k, v, u, z = jnp.split(proj, splits, axis=-1)
        attn = dilated_attention(q, k, v)
        sgu = spatial_gating(u, z, sgu_ln_g[i], sgu_ln_b[i], w_spatial[i], b_spatial[i])
        groups = jnp.concatenate([rmsnorm(attn, attn_out_norm[i]),
                                  rmsnorm(sgu, sgu_out_norm[i])], axis=-1)
        mixed = groups @ w_out[i]
        h = h + rmsnorm(mixed, ln_post_mix[i])
        f = rmsnorm(h, ln_pre_ffn[i])
        g, up = jnp.split(f @ w_gate_up[i], 2, axis=-1)
        y = (jax.nn.silu(g) * up) @ w_down[i]
        h = h + rmsnorm(y, ln_post_ffn[i])
        gate = jax.nn.sigmoid(h @ w_pe_gate[i] + b_pe_gate[i])
        h = h + gate * (p[i] @ w_pe_proj[i])
    return h


DEPTH_2 = 2

N_MIXERS = 2
N_A_LAYERS = (DEPTH_2 + 1) // 2
N_B_LAYERS = DEPTH_2 // 2
Q_BLOCK = 128

SB_HEADS = 16
SB_HEAD_DIM = D_MODEL // SB_HEADS

DSA_HEADS = 16
DSA_LATENT = 128
DSA_V_DIM = D_MODEL // DSA_HEADS
IDX_HEADS = 8
IDX_DIM = 64
TOPK_MAX = 256
DSA_IN = DSA_HEADS * DSA_LATENT + DSA_LATENT + IDX_HEADS * IDX_DIM + IDX_DIM + IDX_HEADS

NUM_BUCKETS = 32
MAX_DISTANCE = 128

FFN_DIM = 2816
CONV_W = 3

RMS_EPS = 1e-6
NEG_2 = -1e30


def rms_norm(x, g):
    xf = x.astype(jnp.float32)
    y = xf * lax.rsqrt(jnp.mean(xf * xf, axis=-1, keepdims=True) + RMS_EPS)
    return (y * g.astype(jnp.float32)).astype(x.dtype)

def _blocks(a):
    B, S = a.shape[0], a.shape[1]
    a = a.reshape((B, S // Q_BLOCK, Q_BLOCK) + a.shape[2:])
    return jnp.moveaxis(a, 1, 0)

def _unblocks(a):
    a = jnp.moveaxis(a, 0, 1)
    return a.reshape((a.shape[0], a.shape[1] * a.shape[2]) + a.shape[3:])

def t5_bucket(dist):
    n = jnp.maximum(dist, 0)
    max_exact = NUM_BUCKETS // 2
    nf = jnp.maximum(n, 1).astype(jnp.float32)
    large = max_exact + (jnp.log(nf / max_exact) / math.log(MAX_DISTANCE / max_exact)
                         * (NUM_BUCKETS - max_exact)).astype(jnp.int32)
    large = jnp.minimum(large, NUM_BUCKETS - 1)
    return jnp.where(n < max_exact, n, large)

def stick_breaking_attention(h, w_in, w_out):
    B, S, _ = h.shape
    qkv = h @ w_in
    q, k, v = jnp.split(qkv, 3, axis=-1)
    q = q.reshape(B, S, SB_HEADS, SB_HEAD_DIM).astype(jnp.float32) * (SB_HEAD_DIM ** -0.5)
    k = k.reshape(B, S, SB_HEADS, SB_HEAD_DIM).astype(jnp.float32)
    v = v.reshape(B, S, SB_HEADS, SB_HEAD_DIM).astype(jnp.float32)
    key_pos = jnp.arange(S)

    def block(args):
        qb, t0 = args
        t = t0 + jnp.arange(Q_BLOCK)
        z = jnp.einsum('bqhd,bshd->bhqs', qb, k)
        strict = key_pos[None, :] < t[:, None]
        log_keep = jnp.where(strict, jax.nn.log_sigmoid(-z), 0.0)
        suffix = lax.cumsum(log_keep, axis=3, reverse=True) - log_keep
        a = jnp.where(strict, jnp.exp(jax.nn.log_sigmoid(z) + suffix), 0.0)
        return jnp.einsum('bhqs,bshd->bqhd', a, v)

    starts = jnp.arange(S // Q_BLOCK) * Q_BLOCK
    o = _unblocks(lax.map(block, (_blocks(q), starts)))
    return o.reshape(B, S, SB_HEADS * SB_HEAD_DIM).astype(h.dtype) @ w_out

def dsa_attention(h, w_in, q_gain, k_gain, w_uv, w_out, rel_bias):
    B, S, _ = h.shape
    topk = min(TOPK_MAX, S // 4)
    proj = h @ w_in
    o1 = DSA_HEADS * DSA_LATENT
    o2 = o1 + DSA_LATENT
    o3 = o2 + IDX_HEADS * IDX_DIM
    o4 = o3 + IDX_DIM
    q, lat, qi, ki, wi = jnp.split(proj, [o1, o2, o3, o4], axis=-1)
    q = rms_norm(q.reshape(B, S, DSA_HEADS, DSA_LATENT), q_gain).astype(jnp.float32)
    k = rms_norm(lat, k_gain).astype(jnp.float32)
    vals = lat.astype(jnp.float32)
    qi = qi.reshape(B, S, IDX_HEADS, IDX_DIM).astype(jnp.float32)
    ki = ki.astype(jnp.float32)
    wi = wi.astype(jnp.float32) * (IDX_HEADS ** -0.5)
    bidx = jnp.arange(B)[:, None, None]
    key_pos = jnp.arange(S)
    scale = DSA_LATENT ** -0.5

    def block(args):
        qb, qib, wib, t0 = args
        t = t0 + jnp.arange(Q_BLOCK)
        isc = jax.nn.relu(jnp.einsum('bqhd,bsd->bqhs', qib, ki))
        isc = jnp.einsum('bqhs,bqh->bqs', isc, wib)
        causal = key_pos[None, :] <= t[:, None]
        isc = jnp.where(causal[None], isc, NEG_2)
        _, sel = lax.top_k(isc, topk)
        valid = sel <= t[None, :, None]
        kg = k[bidx, sel]
        vg = vals[bidx, sel]
        logits = jnp.einsum('bqhd,bqkd->bqhk', qb, kg) * scale
        bias = rel_bias[t5_bucket(t[None, :, None] - sel)]
        logits = logits + jnp.swapaxes(bias, -1, -2).astype(jnp.float32)
        logits = jnp.where(valid[:, :, None, :], logits, NEG_2)
        p = jax.nn.softmax(logits, axis=-1)
        return jnp.einsum('bqhk,bqkd->bqhd', p, vg)

    starts = jnp.arange(S // Q_BLOCK) * Q_BLOCK
    o_lat = _unblocks(lax.map(block, (_blocks(q), _blocks(qi), _blocks(wi), starts)))
    o = jnp.einsum('bshl,hlv->bshv', o_lat, w_uv.astype(jnp.float32))
    return o.reshape(B, S, DSA_HEADS * DSA_V_DIM).astype(h.dtype) @ w_out

def conv_ffn(h, w_up, conv_w, conv_b, w_down):
    S = h.shape[1]
    u = h @ w_up
    up = jnp.pad(u, ((0, 0), (CONV_W - 1, 0), (0, 0)))
    y = conv_b
    for j in range(CONV_W):
        y = y + up[:, j:j + S] * conv_w[j]
    gate, val = jnp.split(y, 2, axis=-1)
    return (jax.nn.silu(gate) * val) @ w_down

def second_inputs(seed: int = 0) -> dict:
    key = jax.random.key(seed)
    ks = jax.random.split(key, 20)
    f32 = jnp.float32
    D = D_MODEL

    def nrm(k, shape, s):
        return jax.random.normal(k, shape, f32) * s

    return {
        'x': nrm(ks[0], (BATCH, SEQ, D), 1.0),
        'c': nrm(ks[1], (BATCH, D), 1.0),
        'ada_w': nrm(ks[2], (DEPTH_2, D, 6 * D), 0.5 * D ** -0.5),
        'ada_b': nrm(ks[3], (DEPTH_2, 6 * D), 0.01),
        'norm_mix': 1.0 + nrm(ks[4], (DEPTH_2, D), 0.05),
        'norm_ffn': 1.0 + nrm(ks[5], (DEPTH_2, D), 0.05),
        'sb_w_in': nrm(ks[6], (N_A_LAYERS, D, 3 * SB_HEADS * SB_HEAD_DIM), D ** -0.5),
        'sb_w_out': nrm(ks[7], (N_A_LAYERS, SB_HEADS * SB_HEAD_DIM, D), (SB_HEADS * SB_HEAD_DIM) ** -0.5),
        'dsa_w_in': nrm(ks[8], (N_B_LAYERS, D, DSA_IN), D ** -0.5),
        'dsa_q_norm': 1.0 + nrm(ks[9], (N_B_LAYERS, DSA_LATENT), 0.05),
        'dsa_k_norm': 1.0 + nrm(ks[10], (N_B_LAYERS, DSA_LATENT), 0.05),
        'dsa_w_uv': nrm(ks[11], (N_B_LAYERS, DSA_HEADS, DSA_LATENT, DSA_V_DIM), DSA_LATENT ** -0.5),
        'dsa_w_out': nrm(ks[12], (N_B_LAYERS, DSA_HEADS * DSA_V_DIM, D), (DSA_HEADS * DSA_V_DIM) ** -0.5),
        'rel_bias': nrm(ks[13], (NUM_BUCKETS, DSA_HEADS), 0.5),
        'ffn_w_up': nrm(ks[14], (DEPTH_2, D, 2 * FFN_DIM), D ** -0.5),
        'ffn_conv_w': nrm(ks[15], (DEPTH_2, CONV_W, 2 * FFN_DIM), CONV_W ** -0.5),
        'ffn_conv_b': nrm(ks[16], (DEPTH_2, 2 * FFN_DIM), 0.01),
        'ffn_w_down': nrm(ks[17], (DEPTH_2, FFN_DIM, D), FFN_DIM ** -0.5),
    }

def second_block(x, c, ada_w, ada_b, norm_mix, norm_ffn, sb_w_in, sb_w_out, dsa_w_in,
              dsa_q_norm, dsa_k_norm, dsa_w_uv, dsa_w_out, rel_bias, ffn_w_up,
              ffn_conv_w, ffn_conv_b, ffn_w_down):
    cond = jax.nn.silu(c)
    for i in range(DEPTH_2):
        mod = cond @ ada_w[i] + ada_b[i]
        sh1, sc1, g1, sh2, sc2, g2 = [m[:, None, :] for m in jnp.split(mod, 6, axis=-1)]
        h = rms_norm(x, norm_mix[i]) * (1.0 + sc1) + sh1
        j = i // N_MIXERS
        if i % N_MIXERS == 0:
            mix = stick_breaking_attention(h, sb_w_in[j], sb_w_out[j])
        else:
            mix = dsa_attention(h, dsa_w_in[j], dsa_q_norm[j], dsa_k_norm[j],
                                dsa_w_uv[j], dsa_w_out[j], rel_bias)
        x = x + g1 * mix
        h = rms_norm(x, norm_ffn[i]) * (1.0 + sc2) + sh2
        x = x + g2 * conv_ffn(h, ffn_w_up[i], ffn_conv_w[i], ffn_conv_b[i], ffn_w_down[i])
    return x


def setup_inputs(seed=0):
    out = dict(first_inputs(seed))
    for name, value in second_inputs(seed + 1).items():
        if name != "x":
            out[name + "_2"] = value
    return out


def reference(
    x, p, ln_pre_mix, w_in, sgu_ln_g, sgu_ln_b, w_spatial, b_spatial, attn_out_norm,
    sgu_out_norm, w_out, ln_post_mix, ln_pre_ffn, w_gate_up, w_down, ln_post_ffn, w_pe_gate,
    b_pe_gate, w_pe_proj, c_2, ada_w_2, ada_b_2, norm_mix_2, norm_ffn_2, sb_w_in_2, sb_w_out_2,
    dsa_w_in_2, dsa_q_norm_2, dsa_k_norm_2, dsa_w_uv_2, dsa_w_out_2, rel_bias_2, ffn_w_up_2,
    ffn_conv_w_2, ffn_conv_b_2, ffn_w_down_2,
):
    x = first_block(
        x, p, ln_pre_mix, w_in, sgu_ln_g, sgu_ln_b, w_spatial, b_spatial, attn_out_norm,
        sgu_out_norm, w_out, ln_post_mix, ln_pre_ffn, w_gate_up, w_down, ln_post_ffn, w_pe_gate,
        b_pe_gate, w_pe_proj,
    )
    return second_block(
        x, c_2, ada_w_2, ada_b_2, norm_mix_2, norm_ffn_2, sb_w_in_2, sb_w_out_2, dsa_w_in_2,
        dsa_q_norm_2, dsa_k_norm_2, dsa_w_uv_2, dsa_w_out_2, rel_bias_2, ffn_w_up_2,
        ffn_conv_w_2, ffn_conv_b_2, ffn_w_down_2,
    )


_drawn_inputs = setup_inputs


def setup_inputs(seed=0):
    import zlib

    import numpy as np

    out = dict(_drawn_inputs(seed))
    spreads = {}
    factors = {'sgu_ln_g': 3.478,
     'sgu_ln_b': 6.822,
     'b_pe_gate': 8.0,
     'ada_b_2': 6.372,
     'norm_mix_2': 6.356,
     'norm_ffn_2': 4.896,
     'dsa_q_norm_2': 8.0,
     'dsa_k_norm_2': 8.0,
     'rel_bias_2': 5.067,
     'ffn_conv_b_2': 8.0}
    for name, (base, spread) in spreads.items():
        noise = np.random.default_rng([zlib.crc32(name.encode()), seed]).standard_normal(out[name].shape)
        drawn = base * np.exp(spread * noise) if base else spread * noise
        out[name] = __import__('jax').numpy.asarray(drawn.astype(out[name].dtype))
    for name, factor in factors.items():
        out[name] = (out[name] * factor).astype(out[name].dtype)
    return out
```

```python
from contextlib import ExitStack
import math

import numpy as np
import concourse.bass as bass
from concourse import mybir

F32 = mybir.dt.float32
F32R = mybir.dt.float32r
BF16 = mybir.dt.bfloat16
U32 = mybir.dt.uint32
ACT = mybir.ActivationFunctionType
ALU = mybir.AluOpType

P = 128
S = 512
D = 1024
DC = D // P
TT = S // P
ATT = 512
A_HEADS, A_HD = 8, 64
GROUPS = 4
FF = 2816
FC = FF // P
PLE = 256
B_HEADS, B_HD = 16, 64
D_HEADS, D_LAT, D_V = 16, 128, 64
IDX_HEADS, IDX_DIM = 8, 64
TOPK = 128
BUCKETS, MAX_DIST = 32, 128
EPS = 1e-6
NEG = -1e30
TAKEN = -3e38
BLOCK = D
RAW = 4
SPLIT = 2
MOD = 6 * DC
SPAN = 640
ADA_STEP = 8

PHASES = [("z", 4), ("u", 4), ("q", 4), ("k", 4), ("v", 4), ("out1", 8), ("gu1", 2 * FC), ("down1", FC),
          ("pe_proj", 2), ("pe_gate", 8),
          ("bq", 8), ("bk", 8), ("bv", 8), ("out2", 8), ("gu2", 2 * FC), ("down2", FC),
          ("qi", 4), ("ki", 1), ("lat", 1), ("dq", 16), ("uv", 1), ("out3", 8), ("gu3", 2 * FC), ("down3", FC)]
START, _n = {}, 0
for _name, _count in PHASES:
    START[_name] = _n
    _n += _count
N_BLOCKS = _n
COUNT = dict(PHASES)

TILES = [("z", "act", 4), ("u", "act", 4), ("q", "act", 4), ("k", "act", 4), ("v", "act", 4), ("out1", "act", 8),
         ("gu1", "dve", 44), ("pe_proj", "act", 8), ("pe_gate", "act", 8), ("bq", "act", 8), ("bk", "act", 8),
         ("bv", "act", 8), ("out2", "x", 8), ("gu2", "dve", 44), ("qi", "act", 4), ("ki", "act", 1),
         ("lat", "dve", 1), ("dq", "dve", 16), ("uv", "act", 8), ("out3", "x", 8), ("gu3", "dve", 44)]
FREED, _t = {}, {"act": 0, "dve": 0, "x": 0}
for _name, _eng, _count in TILES:
    FREED[_name] = (_eng, dict(_t))
    _t[_eng] += _count
FREED["end"] = ("act", dict(_t))

SPLITS = [("pre_mix", 8), ("sgu", 4), ("attn", 4), ("pre_ffn", 8), ("down1", FC), ("p", 2), ("pe_gate", 8), ("mix0", 8),
          ("battn", 8), ("ffn0", 8), ("down2", FC), ("mix1", 8), ("dattn", 8), ("ffn1", 8), ("down3", FC)]
SPLIT_AT, _n = {}, 0
for _name, _count in SPLITS:
    SPLIT_AT[_name] = _n
    _n += _count

NORMS = {"pre_mix": (0, 0), "sgu": (8, 1), "attn": (12, 2), "post_mix": (16, 3), "pre_ffn": (24, 4),
         "post_ffn": (32, 5), "mix0": (40, 6), "ffn0": (48, 7), "mix1": (56, 8), "ffn1": (64, 9)}
X_AT = {"post_mix": 0, "post_ffn": 8, "pe_gate": 16, "out2": 24, "down2": 32, "out3": 40, "down3": 48}
T_AT = {"pre_mix": 0, "sgu": 8, "attn": 12, "pre_ffn": 16, "mix0": 24, "ffn0": 32, "mix1": 40, "ffn1": 48}

VECS = [("ln_pre_mix", 8), ("attn_out_norm", 4), ("sgu_out_norm", 4), ("ln_post_mix", 8), ("ln_pre_ffn", 8),
        ("ln_post_ffn", 8), ("b_pe_gate", 8), ("norm_mix_2", 16), ("norm_ffn_2", 16), ("ada_b_2", 2 * MOD),
        ("dsa_q_norm_2", 1), ("dsa_k_norm_2", 1), ("conv", 2 * FC * 8)]
VEC, _n = {}, 0
for _name, _count in VECS:
    VEC[_name] = _n
    _n += _count
N_VECS = _n
CONSTS = ["ident", "ones", "neg_ones", "neg_suffix", "upper", "causal", "strict"]


def two_blocks(nc, x_in, p_in, vecs_in, stream_in, ada_in, consts_in, bias_in, onehot_in, rel_in, wi_in,
               sgu_g_in, sgu_b_in, bs_in, ws_in, c_in, scratch, out):
    ctx = ExitStack()

    def sb(name, shape, dt=F32, stack=None):
        return (stack or ctx).enter_context(nc.sbuf_tensor(name, shape, dt))

    def sem(name):
        return ctx.enter_context(nc.semaphore(name))

    with ctx:
        x = sb("x", [P, DC, S])
        a_hi = sb("a_hi", [P, DC, S], F32R)
        a_lo = sb("a_lo", [P, DC, S], F32R)
        raw = sb("raw", [P, RAW, BLOCK])
        w_hi = sb("w_hi", [P, SPLIT, BLOCK], F32R)
        w_lo = sb("w_lo", [P, SPLIT, BLOCK], F32R)
        big = sb("big", [P, 24, S])
        tmp = sb("tmp", [P, 4, S])
        y = sb("y", [P, DC, S])
        bias = sb("bias", [P, DC, S])
        squares = sb("squares", [P, 2, S])
        sq_sum = sb("sq_sum", [P, S])
        var = sb("var", [P, S])
        rstd = sb("rstd", [P, S])
        vecs = sb("vecs", [P, N_VECS])
        consts = sb("consts", [P, len(CONSTS), P])
        ident_b = sb("ident_b", [P, P], BF16)
        strict_b = sb("strict_b", [P, P], BF16)
        neg_ones_r = sb("neg_ones_r", [P, P], F32R)
        neg_suffix_r = sb("neg_suffix_r", [P, P], F32R)
        mods = sb("mods", [P, 2 * MOD])
        gains = sb("gains", [P, 4, DC])
        kq_gain = sb("kq_gain", [P, 1])
        ada_part = sb("ada_part", [P, ADA_STEP])
        n_stat = 2 * D_HEADS * TT
        neg_max = sb("neg_max", [P, n_stat])
        den = sb("den", [P, n_stat])
        rden = sb("rden", [P, n_stat])
        z_stat = sb("z_stat", [P, 16, 6])
        z_mv = sb("z_mv", [P, 16, 2])
        z_rstd = sb("z_rstd", [P, 16])
        wi_raw = sb("wi_raw", [P, DC * IDX_HEADS])
        wi_hi = sb("wi_hi", [P, DC, IDX_HEADS], F32R)
        wi_lo = sb("wi_lo", [P, DC, IDX_HEADS], F32R)
        wi = sb("wi", [P, TT, IDX_HEADS])
        top8 = sb("top8", [P, 8])
        with ExitStack() as first:
            sgu_g = sb("sgu_g", [P, P], F32, first)
            sgu_b = sb("sgu_b", [P, P], F32, first)
            bs = sb("bs", [P, GROUPS, P], F32, first)
            ws = sb("ws", [P, GROUPS, P], F32, first)
        with ExitStack() as second:
            probs_t = sb("probs_t", [P, 4, S], F32, second)
            ctx.push(second.pop_all())
        with ExitStack() as first:
            cond = sb("cond", [P, D], F32, first)
        with ExitStack() as second:
            k_lat = sb("k_lat", [P, S], F32, second)
            lat_hi = sb("lat_hi", [P, S], F32R, second)
            lat_lo = sb("lat_lo", [P, S], F32R, second)
            not_selected = sb("not_selected", [P, TT, S], BF16, second)
            ctx.push(second.pop_all())

        bank = [ctx.enter_context(nc.psum_tensor(f"bank{i}", [P, S], F32)) for i in range(8)]
        sum_bank = bank[4]

        ident = consts[:, 0, :]
        ones = consts[:, 1, :]
        neg_ones = consts[:, 2, :]
        neg_suffix = consts[:, 3, :]
        upper = consts[:, 4, :]
        causal = consts[:, 5, :]
        strict = consts[:, 6, :]

        def vec(name, c, n=1):
            return vecs[:, VEC[name] + c:VEC[name] + c + n]

        def mod(layer, which, c):
            return mods[:, layer * MOD + which * DC + c:layer * MOD + which * DC + c + 1]

        def f32(ap):
            return ap.bitcast(F32)

        raw_landed = [sem(f"raw_landed{j}") for j in range(RAW)]
        zeroed = sem("zeroed")
        split_begun = sem("split_begun")
        high_ready = sem("high_ready")
        split_ready = sem("split_ready")
        block_done = sem("block_done")
        banks_free = {"act": sem("banks_free_act"), "dve": sem("banks_free_dve")}
        down_done = sem("down_done")
        down_taken = sem("down_taken")
        vecs_landed, consts_landed, x_landed, bias_landed = sem("vecs_landed"), sem("consts_landed"), sem("x_landed"), sem("bias_landed")
        rows_landed, cond_landed, p_landed, wi_landed = sem("rows_landed"), sem("cond_landed"), sem("p_landed"), sem("wi_landed")
        onehot_landed = sem("onehot_landed")
        masks_ready = sem("masks_ready")
        sq_ready, sq_added, sum_ready = sem("sq_ready"), sem("sq_added"), sem("sum_ready")
        var_ready, rstd_ready = sem("var_ready"), sem("rstd_ready")
        scaled_ready, hi_ready, lo_ready = sem("scaled_ready"), sem("hi_ready"), sem("lo_ready")
        x_ready = sem("x_ready")
        z_step, z_std, z_normed = sem("z_step"), sem("z_std"), sem("z_normed")
        ws_masked = sem("ws_masked")
        mixed_ready, mixed_step, sgu_ready = sem("mixed_ready"), sem("mixed_step"), sem("sgu_ready")
        post_step = sem("post_step")
        silu_ready, conv_base, conv_step, hidden_ready = sem("silu_ready"), sem("conv_base"), sem("conv_step"), sem("hidden_ready")
        cond_ready, ada_done, ada_copied, mods_ready = sem("cond_ready"), sem("ada_done"), sem("ada_copied"), sem("mods_ready")
        ada_landed = [sem(f"ada_landed{j}") for j in range(4)]
        pe_ready, gate_ready, gate_step = sem("pe_ready"), sem("gate_ready"), sem("gate_step")
        index_init = sem("index_init")
        rel_row, rel_copied, rel_stored, tables_landed = sem("rel_row"), sem("rel_copied"), sem("rel_stored"), sem("tables_landed")
        out_stored = sem("out_stored")

        wi_split, wi_ready, wi_taken = sem("wi_split"), sem("wi_ready"), sem("wi_taken")
        relu_ready, index_ready, index_added = sem("relu_ready"), sem("index_ready"), sem("index_added")
        qsq_ready, qvar_ready, qsum_ready, qrstd_ready = sem("qsq_ready"), sem("qvar_ready"), sem("qsum_ready"), sem("qrstd_ready")
        lat_split, uv_ready, selected, top_step = sem("lat_split"), sem("uv_ready"), sem("selected"), sem("top_step")

        def freed(name, n):
            eng, before = FREED[name]
            if eng == "x":
                return x_ready, X_AT[name] + n
            return banks_free[eng], 4 + before[eng] + n

        def pe_begin(pe, name):
            before = FREED[name][1]
            pe.wait_ge(banks_free["act"], 4 + before["act"])
            pe.wait_ge(banks_free["dve"], 4 + before["dve"])

        def pe_three_passes(pe, o, lhs_hi, lhs_lo, rhs_hi, rhs_lo, start, stop, **kw):
            pe.matmul(o, lhs_hi, rhs_hi, start=start, stop=False, **kw)
            pe.matmul(o, lhs_hi, rhs_lo, start=False, stop=False, **kw)
            return pe.matmul(o, lhs_lo, rhs_hi, start=False, stop=stop, **kw)

        def pe_tile(pe, name, j, i, chunks_from=None, first_bank=0):
            s = (START[name] + j) % SPLIT
            pe.wait_ge(split_ready, START[name] + 1 + i)
            counter, value = freed(name, i - 3)
            pe.wait_ge(counter, value)
            order = (4, 5, 6, 7, 0, 1, 2, 3) if name == "out1" else range(DC)
            for n, k in enumerate(order):
                if chunks_from is not None:
                    pe.wait_ge(lo_ready, chunks_from + n + 1)
                m = pe_three_passes(pe, bank[(j + first_bank) % 4][:], w_hi[:, s, k * P:(k + 1) * P], w_lo[:, s, k * P:(k + 1) * P],
                                    a_hi[:, k, :], a_lo[:, k, :], n == 0, n == DC - 1)
            m.then_inc(block_done, 1)

        def pe_tiles(pe, name, chunks_from=None):
            n = COUNT[name]
            pe_begin(pe, name)
            if chunks_from is not None:
                for j in range(4):
                    pe_tile(pe, name, j, j, chunks_from if j == 0 else None)
            done = 4 if chunks_from is not None else 0
            if (n - done) // 4 > 1:
                with pe.Fori(done // 4, n // 4) as r:
                    for j in range(4):
                        pe_tile(pe, name, j, r * 4 + j)
                done = n // 4 * 4
            for i in range(done, n):
                pe_tile(pe, name, i % 4, i)

        def pe_token_tiles(pe, name, halves=1):
            pe_begin(pe, name)
            for h in range(halves):
                for b in range(4):
                    i = 4 * h + b
                    s = (START[name] + i) % SPLIT
                    pe.wait_ge(split_ready, START[name] + i + 1)
                    for t in range(TT):
                        if h and b == 0:
                            pe.wait_ge(*freed(name, t + 1))
                        for k2 in range(2):
                            k = 2 * b + k2
                            hi, lo = w_hi[:, s, k2 * S:(k2 + 1) * S], w_lo[:, s, k2 * S:(k2 + 1) * S]
                            xh, xl = a_hi[:, k, t * P:(t + 1) * P], a_lo[:, k, t * P:(t + 1) * P]
                            if name == "z" and t == 0:
                                pe.wait_ge(lo_ready, SPLIT_AT["pre_mix"] + k + 1)
                            m = pe_three_passes(pe, bank[t][:], xh, xl, hi, lo, k == 0, k == DC - 1)
                    m.then_inc(block_done, 1)

        def pe_sum(pe, squares_added, s):
            pe.wait_ge(sq_added, squares_added)
            pe.matmul(sum_bank[:], ones, sq_sum[:], start=True, stop=True).then_inc(sum_ready, 1)

        def pe_down(pe, name, n):
            pe_begin(pe, {"down1": "pe_proj", "down2": "qi", "down3": "end"}[name])

            def chunk(j, i, start=False, stop=False):
                s = (START[name] + j) % SPLIT
                pe.wait_ge(split_ready, START[name] + 1 + i)
                pe.wait_ge(lo_ready, SPLIT_AT[name] + 1 + i)
                for c in range(DC):
                    m = pe_three_passes(pe, bank[c][:], w_hi[:, s, c * P:(c + 1) * P], w_lo[:, s, c * P:(c + 1) * P],
                                        a_hi[:, j, :], a_lo[:, j, :], start, stop, skip_group_check=True)
                    if stop and c < DC - 1:
                        m.then_inc(down_done, 1)
                m.then_inc(block_done, 1)
            for j in range(4):
                chunk(j, j, start=j == 0)
            with pe.Fori(1, FC // 4) as r:
                for j in range(4):
                    chunk(j, r * 4 + j)
            for i in range(FC // 4 * 4, FC):
                chunk(i % 4, i, stop=i == FC - 1)

        def attention(name, heads):
            sems = {k: sem(f"{name}_{k}") for k in
                    ("scores", "masked", "exp", "rden", "normed", "turned", "copied", "out", "evac")}
            units = [(h, i) for h in range(heads) for i in range(TT)]
            return sems, units

        a_sems, a_units = attention("a", A_HEADS)
        d_sems, d_units = attention("d", D_HEADS)

        def out_bank(h):
            return bank[6 + (h // 2) % 2]

        def pe_attention(pe, sems, units, queries, keys, values, probs, mask, evacuated):
            n = len(units)
            for step in range(n + 3):
                if step < n:
                    h, i = units[step]
                    cols = P * (i + 1)
                    if step >= 3:
                        pe.wait_ge(sems["masked"], step - 2)
                    b = bank[step % 3]
                    m = pe.matmul(b[:, 0:cols], queries(h, i), keys(h, cols), start=True, stop=mask is None)
                    if mask is not None:
                        m = pe.matmul(b[:, 0:cols], ident_b[:], mask(i, cols), start=False, stop=True)
                    m.then_inc(sems["scores"], 1)
                if 2 <= step < n + 2:
                    u = step - 2
                    h, i = units[u]
                    pe.wait_ge(sems["normed"], u + 1)
                    if u >= 2:
                        pe.wait_ge(sems["copied"], u - 1)
                    for j in range(i + 1):
                        m = pe.transpose(bank[(3, 5)[u % 2]][:, j * P:(j + 1) * P], tmp[:, u % 4, j * P:(j + 1) * P], ident)
                    m.then_inc(sems["turned"], 1)
                if step >= 3:
                    u = step - 3
                    h, i = units[u]
                    pe.wait_ge(sems["copied"], u + 1)
                    if h >= 4 and h % 2 == 0 and i == 0:
                        pe.wait_ge(*evacuated(h // 2 - 2))
                    o = out_bank(h)[64 * (h % 2):64 * (h % 2) + 64, i * P:(i + 1) * P]
                    for j in range(i + 1):
                        m = pe.matmul(o, values(h, j), probs(u)[:, j * P:(j + 1) * P], start=j == 0, stop=j == i)
                    m.then_inc(sems["out"], 1)

        def dve_attention(v, sems, units, tables, base, low=None):
            for step in range(len(units) + 5):
                if low is not None and step >= 5 and units[step - 5][0] % 2 and units[step - 5][1] == TT - 1:
                    low(v, units[step - 5][0] // 2)
                if step < len(units):
                    u = step
                    h, i = units[u]
                    cols = P * (i + 1)
                    v.wait_ge(sems["scores"], u + 1)
                    if u >= 4:
                        v.wait_ge(sems["turned"], u - 3)
                    v.tensor_tensor_reduce(tmp[:, u % 4, 0:cols], bank[u % 3][:, 0:cols], tables(h, cols),
                                           -1.0, 3e38, ALU.add, ALU.min, neg_max[:, base + u:base + u + 1]).then_inc(sems["masked"], 1)
                if 1 <= step <= len(units):
                    u = step - 1
                    h, i = units[u]
                    cols = P * (i + 1)
                    v.wait_ge(sems["exp"], u + 1)
                    v.reciprocal(rden[:, base + u:base + u + 1], den[:, base + u:base + u + 1]).then_inc(sems["rden"], 1)
                    v.wait_ge(sems["rden"], u + 1)
                    v.tensor_scalar(tmp[:, u % 4, 0:cols], tmp[:, u % 4, 0:cols], rden[:, base + u:base + u + 1], None,
                                    ALU.mult).then_inc(sems["normed"], 1)

        def act_attention(a, sems, units, probs, base, evacuate):
            for step in range(len(units) + 3):
                if step < len(units):
                    u = step
                    h, i = units[u]
                    cols = P * (i + 1)
                    a.wait_ge(sems["masked"], u + 1)
                    a.activation(tmp[:, u % 4, 0:cols], tmp[:, u % 4, 0:cols], ACT.Exp, bias=neg_max[:, base + u:base + u + 1],
                                 scale=-1.0, accum_out=den[:, base + u:base + u + 1]).then_inc(sems["exp"], 1)
                if 1 <= step <= len(units):
                    u = step - 1
                    h, i = units[u]
                    cols = P * (i + 1)
                    a.wait_ge(sems["turned"], u + 1)
                    if u >= 4:
                        a.wait_ge(sems["out"], u - 3)
                    a.activation(probs(u)[:, 0:cols], bank[(3, 5)[u % 2]][:, 0:cols], ACT.Copy).then_inc(sems["copied"], 1)
                if step >= 3:
                    u = step - 3
                    h, i = units[u]
                    if h % 2 and i == TT - 1:
                        a.wait_ge(sems["out"], u + 1)
                        evacuate(a, h // 2)

        b_z, b_neg, b_exp, b_ln, b_sp, b_hi, b_lo, b_e, b_a, b_out, b_evac = (
            sem(f"b_{k}") for k in ("scores", "neg_abs", "exp", "ln", "softplus", "high", "low", "logits", "weights", "out", "evac"))
        B_PLACE = [(0, 0), (1, 0), (2, 0), (1, 384)]
        B_COLS = [S, S, 256]
        B_ORDER = (1, 2, 0)
        B_TILES = {1: (1, 3), 2: (2,), 0: (0,)}
        y_flat = y[:].rearrange("p c s -> p (c s)")
        bias_flat = bias[:].rearrange("p c s -> p (c s)")
        hi_flat = a_hi[:].rearrange("p c s -> p (c s)")
        lo_flat = a_lo[:].rearrange("p c s -> p (c s)")

        def b_bank(h, n):
            return bank[((0, 1, 2), (3, 5, 6))[h % 2][n]]

        def b_slice(flat, slots, h, n, cols=None, at=0):
            o = (h % slots) * 1280 + n * S + at
            return flat[:, o:o + (B_COLS[n] if cols is None else cols)]

        def soft_buf(h, n):
            return b_slice(y_flat, 3, h, n)

        def sp_high(h, n, cols=None, at=0):
            return b_slice(hi_flat, 2, h, n, cols, at)

        def sp_low(h, n, cols=None, at=0):
            return b_slice(lo_flat, 2, h, n, cols, at)

        def weight_buf(h, n, cols=None, at=0):
            return b_slice(bias_flat, 3, h, n, cols, at)

        def b_values(h, j):
            return (tmp, probs_t)[h // 8][:, j, P * (h % 8 // 2):P * (h % 8 // 2) + P]

        def pe_stick(pe):
            for step in range(B_HEADS + 2):
                if step < B_HEADS:
                    h = step
                    for n in B_ORDER:
                        if h >= 2:
                            pe.wait_ge(b_a, 3 * (h - 2) + B_ORDER.index(n) + 1)
                        for j in B_TILES[n]:
                            at = B_PLACE[j][1]
                            w = S - P * j
                            pe.matmul(b_bank(h, n)[:, at:at + w], big[:, 16 + h // 2, j * P:(j + 1) * P],
                                      big[:, h, j * P:S], start=j != 3, stop=True, skip_group_check=True)
                            m = pe.matmul(b_bank(h, n)[:, at:at + P], ident_b[:], strict_b[:], start=False, stop=True,
                                          skip_group_check=True)
                        m.then_inc(b_z, 1)
                if 1 <= step <= B_HEADS:
                    h = step - 1
                    for n in B_ORDER:
                        pe.wait_ge(b_lo, 3 * h + (3 if n == 0 else 2))
                        for j in B_TILES[n]:
                            at = B_PLACE[j][1]
                            for j2 in range(j, TT):
                                n2, at2 = B_PLACE[j2]
                                w = S - P * j2
                                for part in (sp_high, sp_low):
                                    m = pe.matmul(b_bank(h, n)[:, at + P * (j2 - j):at + P * (j2 - j) + w],
                                                  (neg_suffix_r if j2 == j else neg_ones_r)[:], part(h, n2, w, at2),
                                                  start=False, stop=True, skip_group_check=True)
                        m.then_inc(b_e, 1)
                if step >= 2:
                    h = step - 2
                    pe.wait_ge(b_a, 3 * (h + 1))
                    if h >= 2:
                        pe.wait_ge(b_evac, h - 1)
                    o = bank[(4, 7)[h % 2]]
                    for j in range(TT):
                        n, at = B_PLACE[j]
                        w = S - P * j
                        m = pe.matmul(o[:, P * j:S], b_values(h, j), weight_buf(h, n, w, at), start=j == 0, stop=j == TT - 1)
                    m.then_inc(b_out, 1)

        def dve_stick(v):
            for h in range(B_HEADS):
                if True:
                    for n in B_ORDER:
                        v.wait_ge(b_z, 3 * h + B_ORDER.index(n) + 1)
                        if h >= 3 and n == 1:
                            v.wait_ge(b_lo, 3 * (h - 2))
                        v.tensor_scalar(soft_buf(h, n).bitcast(U32), b_bank(h, n)[:, 0:B_COLS[n]].bitcast(U32), 0x80000000, None,
                                        ALU.bitwise_or).then_inc(b_neg, 1)
                if True:
                    for n in B_ORDER:
                        v.wait_ge(b_ln, 3 * h + B_ORDER.index(n) + 1)
                        v.scalar_tensor_tensor(soft_buf(h, n), b_bank(h, n)[:, 0:B_COLS[n]], 0.0, soft_buf(h, n),
                                               ALU.max, ALU.add).then_inc(b_sp, 1)
                        if h >= 2 and n == 1:
                            v.wait_ge(b_e, 3 * (h - 1))
                        v.wait_ge(b_sp, 3 * h + B_ORDER.index(n) + 1)
                        v.tensor_copy(sp_high(h, n), soft_buf(h, n)).then_inc(b_hi, 1)

        def dve_low_of_bank(v, name, c, b):
            v.wait_ge(hi_ready, SPLIT_AT[name] + c + 1)
            v.tensor_tensor(a_lo[:, c, :], b[:], f32(a_hi[:, c, :]), ALU.subtract).then_inc(lo_ready, 1)

        def act_stick(a):
            for step in range(B_HEADS + 3):
                if step < B_HEADS:
                    h = step
                    for k, n in enumerate(B_ORDER):
                        a.wait_ge(b_neg, 3 * h + k + 1)
                        a.activation(soft_buf(h, n), soft_buf(h, n), ACT.Exp).then_inc(b_exp, 1)
                    for k, n in enumerate(B_ORDER):
                        a.wait_ge(b_exp, 3 * h + k + 1)
                        a.activation(soft_buf(h, n), soft_buf(h, n), ACT.Ln, bias=1.0).then_inc(b_ln, 1)
                if 1 <= step <= B_HEADS:
                    h = step - 1
                    for k, n in enumerate(B_ORDER):
                        a.wait_ge(b_e, 3 * h + k + 1)
                        if h >= 3 and k == 0:
                            a.wait_ge(b_out, h - 2)
                        a.activation(weight_buf(h, n), b_bank(h, n)[:, 0:B_COLS[n]], ACT.Exp).then_inc(b_a, 1)
                if step >= 3:
                    h = step - 3
                    rows = slice(64 * (h % 2), 64 * (h % 2) + 64)
                    a.wait_ge(b_out, h + 1)
                    a.activation(big[rows, h - h % 2, :], bank[(4, 7)[h % 2]][rows, :], ACT.Copy).then_inc(b_evac, 1)

        def act_squares(a, name, srcs, waits):
            k0 = NORMS[name][0]
            for c, src in enumerate(srcs):
                k = k0 + c
                if waits is not None:
                    a.wait_ge(*waits(c))
                if k >= 2:
                    a.wait_ge(sq_added, k - 1)
                a.activation(squares[:, k % 2, :], src, ACT.Square).then_inc(sq_ready, 1)

        def act_rstd(a, s):
            a.wait_ge(var_ready, 2 * s + 2)
            a.activation(rstd[:], var[:], ACT.Sqrt).then_inc(rstd_ready, 1)

        def dve_add_square(v, name, c):
            k0, s = NORMS[name]
            k = k0 + c
            v.wait_ge(sq_ready, k + 1)
            if c == 0:
                if s:
                    v.wait_ge(sum_ready, s)
                v.tensor_copy(sq_sum[:], squares[:, k % 2, :]).then_inc(sq_added, 1)
            else:
                v.wait_ge(sq_added, k)
                v.tensor_tensor(sq_sum[:], sq_sum[:], squares[:, k % 2, :], ALU.add).then_inc(sq_added, 1)

        def dve_var(v, name, width):
            s = NORMS[name][1]
            v.wait_ge(sum_ready, s + 1)
            v.tensor_scalar(var[:], sum_bank[:], 1.0 / width, EPS, ALU.mult, ALU.add).then_inc(var_ready, 1)
            v.wait_ge(var_ready, 2 * s + 1)
            v.reciprocal(var[:], var[:]).then_inc(var_ready, 1)
            v.wait_ge(rstd_ready, s + 1)

        def dve_scale_split(v, name, split, chunks, srcs, gain, shift=None, first=0):
            for c in range(chunks + 1):
                if c < chunks:
                    v.scalar_tensor_tensor(tmp[:, c % 4, :], srcs(c), gain(c), rstd[:], ALU.mult, ALU.mult).then_inc(scaled_ready, 1)
                if c >= 1:
                    e = c - 1
                    v.wait_ge(hi_ready, SPLIT_AT[split] + e + 1)
                    hi, lo = f32(a_hi[:, first + e, :]), a_lo[:, first + e, :]
                    if shift is None:
                        v.tensor_tensor(lo, tmp[:, e % 4, :], hi, ALU.subtract).then_inc(lo_ready, 1)
                    else:
                        v.scalar_tensor_tensor(lo, tmp[:, e % 4, :], shift(e), hi, ALU.add, ALU.subtract).then_inc(lo_ready, 1)

        def act_high(a, name, chunks, shift=None, first=0):
            for c in range(chunks):
                a.wait_ge(scaled_ready, T_AT[name] + c + 1)
                if shift is None:
                    a.activation(a_hi[:, first + c, :], tmp[:, c % 4, :], ACT.Copy).then_inc(hi_ready, 1)
                else:
                    a.activation(a_hi[:, first + c, :], tmp[:, c % 4, :], ACT.Identity, bias=shift(c)).then_inc(hi_ready, 1)

        def act_split_hidden(a, name):
            for t in range(FC):
                if t == 0:
                    a.wait_ge(block_done, START[name])
                if t >= 4:
                    a.wait_ge(block_done, START[name] + t - 3)
                if name == "down1":
                    a.wait_ge(*freed("gu1", 2 * t + 2))
                else:
                    a.wait_ge(hidden_ready, 2 + FC * (name == "down3") + t + 1)
                a.activation(a_hi[:, t % 4, :], big[:, t, :], ACT.Copy).then_inc(hi_ready, 1)

        def dve_split_hidden(v, name):
            for t in range(FC):
                v.wait_ge(hi_ready, SPLIT_AT[name] + t + 1)
                v.tensor_tensor(a_lo[:, t % 4, :], big[:, t, :], f32(a_hi[:, t % 4, :]), ALU.subtract).then_inc(lo_ready, 1)

        def wait_down(e, n, c):
            if c < DC - 1:
                e.wait_ge(down_done, (DC - 1) * n + c + 1)
            else:
                e.wait_ge(block_done, START[("down1", "down2", "down3")[n]] + FC)

        block = ctx.enter_context(nc.Block())

        @block.sync
        def _(sp):
            sp.dma_start(x[:], x_in).then_inc(x_landed, 16)
            sp.dma_start(vecs[:], vecs_in).then_inc(vecs_landed, 16)
            for j in range(RAW):
                sp.dma_start(raw[:, j, :], stream_in[j]).then_inc(raw_landed[j], 16)

            def load(j, b):
                sp.wait_ge(split_ready, b - (RAW - 1))
                sp.dma_start(raw[:, j, :], stream_in[bass.ds(b, 1)].rearrange("o p n -> (o p) n")).then_inc(raw_landed[j], 16)
            with sp.Fori(1, N_BLOCKS // RAW) as r:
                for j in range(RAW):
                    load(j, r * RAW + j)
            for b in range(N_BLOCKS // RAW * RAW, N_BLOCKS):
                load(b % RAW, b)
            for c in range(DC):
                sp.wait_ge(x_ready, X_AT["down3"] + c + 1)
                sp.dma_start(out[:, c, :], x[:, c, :]).then_inc(out_stored, 16)
            sp.wait_ge(out_stored, 16 * DC)

        @block.gpsimd
        def _(pool):
            def split(j, s, b, turn, wait=True):
                pool.wait_ge(raw_landed[j], turn * 16 + 16)
                if wait:
                    pool.wait_ge(block_done, b - (SPLIT - 1))
                pool.sem_inc(split_begun, 1)
                pool.tensor_scalar(w_hi[:, s, :], raw[:, j, :], 1.0, 1.0, ALU.mult, ALU.mult).then_inc(high_ready, 1)
                pool.wait_ge(high_ready, b + 1)
                pool.tensor_tensor(w_lo[:, s, :], raw[:, j, :], f32(w_hi[:, s, :]), ALU.subtract).then_inc(split_ready, 1)

            def split_stream(first, end):
                turns = (end - first) // RAW
                with pool.Fori(0, turns) as r:
                    for j in range(first, first + RAW):
                        split(j % RAW, j % SPLIT, r * RAW + j, r + j // RAW)
                for b in range(first + turns * RAW, end):
                    split(b % RAW, b % SPLIT, b, b // RAW)

            pool.memset(big[64:P, 0:A_HEADS:2, :], 0.0).then_inc(zeroed, 1)
            pool.wait_ge(zeroed, 1)
            pool.memset(big[0:64, 1:A_HEADS:2, :], 0.0).then_inc(zeroed, 1)
            pool.wait_ge(zeroed, 2)
            for b in range(SPLIT):
                split(b, b, b, 0, wait=False)
            split_stream(SPLIT, START["bq"] + SPLIT)
            pool.wait_ge(x_ready, X_AT["pe_gate"] + DC)
            pool.wait_ge(split_ready, START["bq"] + SPLIT)
            pool.memset(big[64:P, 0:B_HEADS:2, :], 0.0).then_inc(zeroed, 1)
            pool.wait_ge(zeroed, 3)
            pool.memset(big[0:64, 1:B_HEADS:2, :], 0.0).then_inc(zeroed, 1)
            pool.wait_ge(zeroed, 4)
            split_stream(START["bq"] + SPLIT, START["out2"] + SPLIT)
            for h in range(B_HEADS):
                for n in (1, 2, 0):
                    pool.wait_ge(b_hi, 3 * h + (1, 2, 0).index(n) + 1)
                    if h >= 2 and n == 1:
                        pool.wait_ge(b_e, 3 * (h - 1))
                    pool.tensor_tensor(sp_low(h, n), soft_buf(h, n), f32(sp_high(h, n)), ALU.subtract).then_inc(b_lo, 1)
            split_stream(START["out2"] + SPLIT, N_BLOCKS)

        @block.tensor
        def _(pe):
            pe.wait_ge(masks_ready, 4)
            pe.wait_ge(onehot_landed, 32)
            big_flat = big[:].rearrange("p c s -> p (c s)")
            for n in range(2):
                m = pe.matmul(bank[5 + n][0:D_HEADS, 0:SPAN // 2], big_flat[0:BUCKETS, 20 * S + SPAN:20 * S + SPAN + D_HEADS],
                              big_flat[0:BUCKETS, 20 * S + n * (SPAN // 2):20 * S + (n + 1) * (SPAN // 2)], start=True, stop=True)
            m.then_inc(rel_row, 1)
            pe_sum(pe, 8, 0)
            pe_token_tiles(pe, "z")
            pe_tiles(pe, "u")
            pe_tiles(pe, "q")
            pe.wait_ge(z_normed, 2 * 16 + TT)
            pe.wait_ge(ws_masked, 1)
            for g in range(GROUPS):
                if g == 3:
                    pe.wait_ge(mixed_step, 1)
                for i in range(TT):
                    m = pe.matmul(bank[5 + g % 3][:, i * P:(i + 1) * P], big[:, 16 + i, g * P:(g + 1) * P], ws[:, g, :],
                                  start=True, stop=True)
                m.then_inc(mixed_ready, 1)
            pe_tiles(pe, "k")
            pe_token_tiles(pe, "v")
            pe_sum(pe, 12, 1)
            pe.wait_ge(*freed("v", 4))
            pe.wait_ge(mixed_step, 4)
            pe.wait_ge(zeroed, 2)
            pe_attention(pe, a_sems, a_units,
                         lambda h, i: big[:, h, i * P:(i + 1) * P],
                         lambda h, cols: big[:, 16 + h // 2, 0:cols],
                         lambda h, j: big[:, 8 + j, h * A_HD:(h + 1) * A_HD],
                         lambda u: y[:, u % 4, :], None, lambda c: (a_sems["evac"], c + 1))
            pe_sum(pe, 16, 2)
            pe_tiles(pe, "out1", SPLIT_AT["sgu"])
            pe_sum(pe, 24, 3)
            pe_sum(pe, 32, 4)
            pe_tiles(pe, "gu1", SPLIT_AT["pre_ffn"])
            pe_down(pe, "down1", 0)
            pe_sum(pe, 40, 5)
            pe.wait_ge(down_taken, 8)
            pe_begin(pe, "pe_proj")
            pe.wait_ge(lo_ready, SPLIT_AT["p"] + 2)
            for b in range(2):
                s = (START["pe_proj"] + b) % SPLIT
                pe.wait_ge(split_ready, START["pe_proj"] + b + 1)
                for t in range(4):
                    pe.wait_ge(*freed("pe_proj", 4 * b + t - 3))
                    for k in range(2):
                        o = (2 * t + k) * P
                        m = pe_three_passes(pe, bank[t][:], w_hi[:, s, o:o + P], w_lo[:, s, o:o + P],
                                            a_hi[:, 4 + k, :], a_lo[:, 4 + k, :], k == 0, k == 1)
                    if t < 3:
                        m.then_inc(pe_ready, 1)
                m.then_inc(block_done, 1)
            pe_tiles(pe, "pe_gate", SPLIT_AT["pe_gate"])
            pe_sum(pe, 48, 6)
            pe_tiles(pe, "bq", SPLIT_AT["mix0"])
            pe_tiles(pe, "bk")
            pe_token_tiles(pe, "bv", 2)
            pe.wait_ge(*freed("bv", 8))
            pe.wait_ge(zeroed, 4)
            pe_stick(pe)
            pe_tiles(pe, "out2", SPLIT_AT["battn"])
            pe_sum(pe, 56, 7)
            pe_tiles(pe, "gu2", SPLIT_AT["ffn0"])
            pe_down(pe, "down2", 1)
            pe_sum(pe, 64, 8)
            pe_tiles(pe, "qi", SPLIT_AT["mix1"])
            pe_tiles(pe, "ki")
            pe.wait_ge(wi_split, 2)
            for t in range(TT):
                for k in range(DC):
                    m = pe_three_passes(pe, bank[7][:, t * 8:(t + 1) * 8], a_hi[:, k, t * P:(t + 1) * P],
                                        a_lo[:, k, t * P:(t + 1) * P], wi_hi[:, k, :], wi_lo[:, k, :], k == 0, k == DC - 1)
            m.then_inc(wi_ready, 1)

            def index_scores(n):
                i, h = 1 + n // IDX_HEADS, n % IDX_HEADS
                cols = P * (i + 1)
                if n == 0:
                    pe.wait_ge(*freed("ki", 1))
                    pe.wait_ge(index_init, 8)
                if n == 2:
                    pe.wait_ge(wi_taken, 1)
                if n >= 3:
                    pe.wait_ge(relu_ready, n - 2)
                pe.matmul(bank[5 + n % 3][:, 0:cols], big[:, 16 + h // 2, i * P:(i + 1) * P], tmp[:, 2 + h % 2, 0:cols],
                          start=True, stop=True).then_inc(index_ready, 1)

            def head_sum(m):
                pe.wait_ge(qsq_ready, m + 1)
                if m:
                    pe.wait_ge(qvar_ready, 2 * m - 1)
                pe.matmul(sum_bank[:], ones, tmp[:, m % 2, :], start=True, stop=True).then_inc(qsum_ready, 1)
            pe_begin(pe, "lat")
            pe_tile(pe, "lat", 0, 0)
            for i in range(D_HEADS):
                pe_tile(pe, "dq", i % 4, i, first_bank=1)
                head_sum(i)
                for n in range(4 * i, min(4 * i + 4, 3 * IDX_HEADS)):
                    index_scores(n)
            head_sum(D_HEADS)
            pe_begin(pe, "uv")
            pe.wait_ge(lat_split, 2)
            s = START["uv"] % SPLIT
            pe.wait_ge(split_ready, START["uv"] + 1)
            for h in range(2):
                for t in range(TT):
                    pe.wait_ge(*freed("uv", 4 * h + t - 3))
                    m = pe_three_passes(pe, bank[t][:], lat_hi[:, t * P:(t + 1) * P], lat_lo[:, t * P:(t + 1) * P],
                                        w_hi[:, s, h * S:(h + 1) * S], w_lo[:, s, h * S:(h + 1) * S], True, True)
                    if h == 0 or t < 3:
                        m.then_inc(uv_ready, 1)
            m.then_inc(block_done, 1)
            pe.wait_ge(*freed("uv", 8))
            pe.wait_ge(selected, 4)
            pe_attention(pe, d_sems, d_units,
                         lambda h, i: big[:, h, i * P:(i + 1) * P],
                         lambda h, cols: k_lat[:, 0:cols],
                         lambda h, j: big[:, 16 + 2 * j + h // 8, 64 * (h % 8):64 * (h % 8) + 64],
                         lambda u: probs_t[:, u % 4, :],
                         lambda i, cols: not_selected[:, i, 0:cols],
                         lambda c: (lo_ready, SPLIT_AT["dattn"] + c + 1))
            pe_tiles(pe, "out3", SPLIT_AT["dattn"])
            pe_sum(pe, 72, 9)
            pe_tiles(pe, "gu3", SPLIT_AT["ffn1"])
            pe_down(pe, "down3", 2)

        def act_tile(a, name, n, b, dst, func=ACT.Copy, **kw):
            a.wait_ge(block_done, b + 1)
            a.activation(dst, bank[n % 4][:], func, **kw).then_inc(banks_free["act"], 1)

        def act_query_pair(a, name, c, scale):
            a.wait_ge(block_done, START[name] + c + 1)
            for half in range(2):
                rows = slice(64 * half, 64 * half + 64)
                m = a.activation(big[rows, 2 * c + half, :], bank[c % 4][rows, :], ACT.Copy, scale=scale)
            m.then_inc(banks_free["act"], 1)

        def ada_load(a, n, m):
            a.dma_start(y_flat[:, m * D:(m + 1) * D], ada_in[bass.ds(n, 1)].rearrange("o p k -> (o p) k")).then_inc(ada_landed[m], 16)

        def act_conv(a, layer):
            phase = "gu2" if layer == 0 else "gu3"
            a.preload_act_table(ACT.Silu)
            with a.Fori(0, FC // 2) as r:
                for jj in range(2):
                    a.wait_ge(hidden_ready, layer * FC + jj + 1 + 2 * r)
                    for g in range(2):
                        n = 2 * jj + g
                        col = VEC["conv"] + (layer * FC + jj) * 8 + 4 * g
                        a.wait_ge(block_done, START[phase] + n + 1 + 4 * r)
                        a.activation(tmp[:, n, :], bank[n][:], ACT.Identity, bias=vecs[:, bass.ds(r * 16 + (col + 3), 1)],
                                     scale=vecs[:, bass.ds(r * 16 + (col + 2), 1)]).then_inc(conv_base, 1)
                    counter, value = freed(phase, 2 * jj + 1)
                    a.wait_ge(counter, value + 4 * r)
                    a.activation(tmp[:, 2 * jj, :], tmp[:, 2 * jj, :], ACT.Silu).then_inc(silu_ready, 1)

        def act_x_squares(a, name, update):
            act_squares(a, name, [x[:, c, :] for c in range(DC)], lambda c: (x_ready, X_AT[update] + c + 1))

        def act_stream_squares(a, name, n, tile_ready, done):
            k0 = NORMS[name][0]
            for c in range(DC):
                tile_ready(c)
                k = k0 + c
                a.wait_ge(sq_added, k - 1)
                b = bank[c % n][:]
                a.activation(squares[:, k % 2, :], b, ACT.Square).then_inc(sq_ready, 1)
                a.activation(y[:, c, :], b, ACT.Copy).then_inc(done, 1)

        @block.scalar
        def _(a):
            a.dma_start(consts[:], consts_in).then_inc(consts_landed, 16)
            a.dma_start(big[0:BUCKETS, 20:22, :].rearrange("p c s -> p (c s)")[:, 0:SPAN], onehot_in).then_inc(onehot_landed, 16)
            a.dma_start(big[0:BUCKETS, 20:22, :].rearrange("p c s -> p (c s)")[:, SPAN:SPAN + D_HEADS], rel_in).then_inc(onehot_landed, 16)
            a.dma_start(sgu_g[:], sgu_g_in.partition_broadcast(P)).then_inc(rows_landed, 16)
            a.dma_start(sgu_b[:], sgu_b_in.partition_broadcast(P)).then_inc(rows_landed, 16)
            a.dma_start(bs[:].rearrange("p g i -> p (g i)"), bs_in.partition_broadcast(P)).then_inc(rows_landed, 16)
            a.dma_start(ws[:], ws_in).then_inc(rows_landed, 16)
            a.dma_start(cond[:], c_in.partition_broadcast(P)).then_inc(cond_landed, 16)
            a.dma_start(wi_raw[:], wi_in).then_inc(wi_landed, 16)
            a.dma_start(bias[:], bias_in).then_inc(bias_landed, 16)
            a.dma_start(big[:, 22:24, :], p_in).then_inc(p_landed, 16)
            a.sem_inc(banks_free["act"], 4)
            a.sem_inc(banks_free["dve"], 4)
            a.sem_inc(hidden_ready, 2)
            act_squares(a, "pre_mix", [x[:, c, :] for c in range(DC)], lambda c: (x_landed, 16))
            act_rstd(a, 0)
            act_high(a, "pre_mix", DC)
            a.wait_ge(rel_row, 1)
            for n in range(2):
                a.activation(y_flat[0:D_HEADS, n * (SPAN // 2):(n + 1) * (SPAN // 2)], bank[5 + n][0:D_HEADS, 0:SPAN // 2],
                             ACT.Copy).then_inc(rel_copied, 1)
            a.wait_ge(rel_copied, 2)
            a.dma_start(scratch, y_flat[0:D_HEADS, 0:SPAN]).then_inc(rel_stored, 16)
            for t in range(TT):
                act_tile(a, "z", t, START["z"] + 3, big[:, 16 + t, :], ACT.Gelu_apprx_tanh)
            for c in range(4):
                act_tile(a, "u", c, START["u"] + c, big[:, 12 + c, :], ACT.Gelu_apprx_tanh)
            a.wait_ge(cond_landed, 16)
            a.activation(cond[:], cond[:], ACT.Silu).then_inc(cond_ready, 1)
            a.wait_ge(rel_stored, 16)
            for n in range(4):
                ada_load(a, n, n)
            a.wait_ge(z_step, 33)
            a.activation(z_rstd[:], z_rstd[:], ACT.Sqrt).then_inc(z_std, 1)
            for c in range(4):
                act_query_pair(a, "q", c, A_HD ** -0.5)
            for n in range(4, ADA_STEP):
                a.wait_ge(ada_done, n - 3)
                ada_load(a, n, n - 4)
            a.wait_ge(mixed_ready, GROUPS)
            for c in range(4):
                act_tile(a, "k", c, START["k"] + c, big[:, 16 + c, :])
            act_squares(a, "sgu", [big[:, 12 + c, :] for c in range(4)], lambda c: (sgu_ready, c + 1))
            for t in range(TT):
                act_tile(a, "v", t, START["v"] + 3, big[:, 8 + t, :])
            act_rstd(a, 1)
            act_high(a, "sgu", 4, first=4)

            def a_evacuate(a, c):
                a.activation(big[:, c, :], bank[6 + c % 2][:], ACT.Copy).then_inc(a_sems["evac"], 1)
            act_attention(a, a_sems, a_units, lambda u: y[:, u % 4, :], 0, a_evacuate)
            act_squares(a, "attn", [big[:, c, :] for c in range(4)], lambda c: (a_sems["evac"], c + 1))
            act_rstd(a, 2)
            act_high(a, "attn", 4)
            act_stream_squares(a, "post_mix", 4, lambda c: a.wait_ge(block_done, START["out1"] + c + 1), banks_free["act"])
            act_rstd(a, 3)
            act_x_squares(a, "pre_ffn", "post_mix")
            act_rstd(a, 4)
            act_high(a, "pre_ffn", DC)
            a.preload_act_table(ACT.Silu)
            with a.Fori(0, FC // 2) as r:
                for jj in range(2):
                    for m in range(4):
                        a.wait_ge(ada_done, r * ADA_STEP + (ADA_STEP + 4 * jj + m - 3))
                        ada_load(a, r * ADA_STEP + (ADA_STEP + 4 * jj + m), m)
                    a.wait_ge(block_done, START["gu1"] + 2 * jj + 1 + 4 * r)
                    a.activation(tmp[:, 2 * jj, :], bank[2 * jj][:], ACT.Silu).then_inc(silu_ready, 1)
            act_split_hidden(a, "down1")
            a.wait_ge(p_landed, 16)
            for k in range(2):
                a.activation(a_hi[:, 4 + k, :], big[:, 22 + k, :], ACT.Copy).then_inc(hi_ready, 1)
            a.wait_ge(ada_done, 2 * MOD)
            act_stream_squares(a, "post_ffn", 8, lambda c: wait_down(a, 0, c), down_taken)
            act_rstd(a, 5)
            for c in range(DC):
                if c % 4 < 3:
                    a.wait_ge(pe_ready, 3 * (c // 4) + c % 4 + 1)
                else:
                    a.wait_ge(block_done, START["pe_proj"] + c // 4 + 1)
                a.activation(big[:, c, :], bank[c % 4][:], ACT.Copy).then_inc(banks_free["act"], 1)
            for c in range(DC):
                a.wait_ge(x_ready, X_AT["post_ffn"] + c + 1)
                a.activation(a_hi[:, c, :], x[:, c, :], ACT.Copy).then_inc(hi_ready, 1)
            for c in range(DC):
                if c >= 4:
                    a.wait_ge(x_ready, X_AT["pe_gate"] + c - 3)
                act_tile(a, "pe_gate", c, START["pe_gate"] + c, tmp[:, c % 4, :], ACT.Sigmoid, bias=vec("b_pe_gate", c))
            act_x_squares(a, "mix0", "pe_gate")
            act_rstd(a, 6)
            a.wait_ge(mods_ready, 1)
            act_high(a, "mix0", DC, shift=lambda c: mod(0, 0, c))
            for c in range(8):
                act_query_pair(a, "bq", c, B_HD ** -0.5)
            for c in range(8):
                act_tile(a, "bk", c, START["bk"] + c, big[:, 16 + c, :])
            for h in range(2):
                for t in range(TT):
                    act_tile(a, "bv", t, START["bv"] + 4 * h + 3, (tmp, probs_t)[h][:, t, :])
            act_stick(a)
            a.wait_ge(b_e, 3 * B_HEADS)
            for c in range(DC):
                a.wait_ge(b_evac, 2 * c + 2)
                a.activation(a_hi[:, c, :], big[:, 2 * c, :], ACT.Copy).then_inc(hi_ready, 1)
            a.wait_ge(b_out, B_HEADS)
            for n, dst in enumerate((y, bias)):
                src = bass.AP(tensor=scratch.tensor, offset=8 * n * SPAN, ap=[[1, P], [SPAN, 8], [1, S]])
                a.dma_start(dst[:], src).then_inc(tables_landed, 16)
            act_x_squares(a, "ffn0", "out2")
            act_rstd(a, 7)
            act_high(a, "ffn0", DC, shift=lambda c: mod(0, 3, c))
            act_conv(a, 0)
            act_split_hidden(a, "down2")
            act_x_squares(a, "mix1", "down2")
            act_rstd(a, 8)
            act_high(a, "mix1", DC, shift=lambda c: mod(1, 0, c))
            for c in range(4):
                act_tile(a, "qi", c, START["qi"] + c, big[:, 16 + c, :])
            a.wait_ge(block_done, START["ki"] + 1)
            a.activation(tmp[0:64, 2, :], bank[0][0:64, :], ACT.Copy)
            a.activation(tmp[64:P, 3, :], bank[0][64:P, :], ACT.Copy).then_inc(banks_free["act"], 1)
            a.wait_ge(wi_ready, 1)
            a.activation(wi[:].rearrange("p t h -> p (t h)"), bank[7][:, 0:TT * IDX_HEADS], ACT.Copy,
                         scale=IDX_HEADS ** -0.5).then_inc(wi_taken, 1)

            def head_square(m):
                b = START["lat"] if m == 0 else START["dq"] + m - 1
                a.wait_ge(block_done, b + 1)
                if m >= 2:
                    a.wait_ge(qsum_ready, m - 1)
                a.activation(tmp[:, m % 2, :], bank[m % 4][:], ACT.Square).then_inc(qsq_ready, 1)

            def head_rstd(m):
                a.wait_ge(qvar_ready, 2 * m + 2)
                if m:
                    a.wait_ge(*freed("lat", m))
                a.activation(rstd[:], var[:], ACT.Sqrt).then_inc(qrstd_ready, 1)

            def index_relu(n):
                cols = P * (2 + n // IDX_HEADS)
                a.wait_ge(index_ready, n + 1)
                if n >= 4:
                    a.wait_ge(index_added, n - 3)
                a.activation(probs_t[:, n % 4, 0:cols], bank[5 + n % 3][:, 0:cols], ACT.Relu).then_inc(relu_ready, 1)
            head_square(0)
            a.activation(lat_hi[:], bank[0][:], ACT.Copy).then_inc(lat_split, 1)
            for m in range(1, D_HEADS + 1):
                head_square(m)
                head_rstd(m - 1)
                for n in range(4 * m - 4, min(4 * m, 3 * IDX_HEADS)):
                    index_relu(n)
            head_rstd(D_HEADS)
            a.wait_ge(selected, 4)
            for h in range(2):
                for t in range(TT):
                    if h == 0 or t < 3:
                        a.wait_ge(uv_ready, 4 * h + t + 1)
                    else:
                        a.wait_ge(block_done, START["uv"] + 1)
                    a.activation(big[:, 16 + 2 * t + h, :], bank[t][:], ACT.Copy).then_inc(banks_free["act"], 1)

            def d_evacuate(a, c):
                a.activation(a_hi[:, c, :], bank[6 + c % 2][:], ACT.Copy).then_inc(hi_ready, 1)
            act_attention(a, d_sems, d_units, lambda u: probs_t[:, u % 4, :], n_stat // 2, d_evacuate)
            act_x_squares(a, "ffn1", "out3")
            act_rstd(a, 9)
            act_high(a, "ffn1", DC, shift=lambda c: mod(1, 3, c))
            act_conv(a, 1)
            act_split_hidden(a, "down3")

        def dve_norm_x(v, name, squares_name=None):
            for c in range(DC):
                dve_add_square(v, name, c)
            dve_var(v, name, D)

        def dve_post_norm(v, name, n):
            g = "ln_" + name
            for c in range(DC + 1):
                if c < DC:
                    v.scalar_tensor_tensor(tmp[:, c % 4, :], y[:, c, :], vec(g, c), rstd[:], ALU.mult, ALU.mult).then_inc(post_step, 1)
                if c >= 1:
                    v.wait_ge(post_step, DC * n + c)
                    v.tensor_tensor(x[:, c - 1, :], x[:, c - 1, :], tmp[:, (c - 1) % 4, :], ALU.add).then_inc(x_ready, 1)

        def dve_ada(v, n, m, part):
            w = y_flat[:, m * D:(m + 1) * D]
            v.tensor_tensor_reduce(w, w, cond[:], 1.0, 0.0, ALU.mult, ALU.add, ada_part[:, part:part + 1]).then_inc(ada_done, 1)

        def dve_conv(v, layer):
            phase = "gu2" if layer == 0 else "gu3"
            with v.Fori(0, FC // 2) as r:
                for jj in range(2):
                    for g in range(2):
                        n = 2 * jj + g
                        col = VEC["conv"] + (layer * FC + jj) * 8 + 4 * g
                        v.wait_ge(conv_base, layer * 2 * FC + n + 1 + 4 * r)
                        v.scalar_tensor_tensor(tmp[:, n, 1:S], bank[n][:, 0:S - 1], vecs[:, bass.ds(r * 16 + (col + 1), 1)],
                                               tmp[:, n, 1:S], ALU.mult, ALU.add).then_inc(conv_step, 1)
                        v.wait_ge(conv_step, layer * 2 * FC + n + 1 + 4 * r)
                        v.scalar_tensor_tensor(tmp[:, n, 2:S], bank[n][:, 0:S - 2], vecs[:, bass.ds(r * 16 + col, 1)],
                                               tmp[:, n, 2:S], ALU.mult, ALU.add).then_inc(banks_free["dve"], 1)
                    counter, value = freed(phase, 2 * jj + 2)
                    v.wait_ge(counter, value + 4 * r)
                    v.wait_ge(silu_ready, FC + layer * FC + jj + 1 + 2 * r)
                    v.tensor_tensor(big[:, bass.ds(r * 2 + jj, 1), :].rearrange("p o s -> p (o s)"), tmp[:, 2 * jj, :],
                                    tmp[:, 2 * jj + 1, :], ALU.mult).then_inc(hidden_ready, 1)

        def dve_residual(v, update, layer, which, ready, n):
            for c in range(DC):
                ready(c)
                v.scalar_tensor_tensor(x[:, c, :], bank[c % n][:], mod(layer, which, c), x[:, c, :], ALU.mult,
                                       ALU.add).then_inc(x_ready, 1)

        @block.vector
        def _(v):
            v.wait_ge(consts_landed, 16)
            v.tensor_copy(ident_b[:], ident).then_inc(masks_ready, 1)
            v.tensor_copy(strict_b[:], strict).then_inc(masks_ready, 1)
            v.tensor_copy(neg_ones_r[:], neg_ones).then_inc(masks_ready, 1)
            v.tensor_copy(neg_suffix_r[:], neg_suffix).then_inc(masks_ready, 1)
            dve_norm_x(v, "pre_mix")
            v.wait_ge(vecs_landed, 16)
            dve_scale_split(v, "pre_mix", "pre_mix", DC, lambda c: x[:, c, :], lambda c: vec("ln_pre_mix", c))
            v.wait_ge(rows_landed, 64)
            v.tensor_tensor(ws[:], ws[:], upper.unsqueeze(1).broadcast_to([P, GROUPS, P]), ALU.mult).then_inc(ws_masked, 1)
            for t in range(TT):
                v.wait_ge(*freed("z", t + 1))
                for g in range(GROUPS):
                    v.bn_stats(z_stat[:, 4 * t + g, :], big[:, 16 + t, g * P:(g + 1) * P]).then_inc(z_step, 1)
            for n in range(16):
                v.wait_ge(z_step, 16)
                v.bn_aggr(z_mv[:, n, :], z_stat[:, n, :]).then_inc(z_normed, 1)
            v.wait_ge(z_normed, 16)
            v.tensor_scalar(z_rstd[:], z_mv[:, :, 1], EPS, None, ALU.add).then_inc(z_step, 16)
            v.wait_ge(z_step, 32)
            v.reciprocal(z_rstd[:], z_rstd[:]).then_inc(z_step, 1)
            v.wait_ge(z_std, 1)
            for n in range(16):
                t, g = n // 4, n % 4
                zg = big[:, 16 + t, g * P:(g + 1) * P]
                v.tensor_scalar(zg, zg, z_mv[:, n, 0:1], z_rstd[:, n:n + 1], ALU.subtract, ALU.mult).then_inc(z_normed, 1)
            for t in range(TT):
                zt = big[:, 16 + t, :].rearrange("p (g i) -> p g i", g=GROUPS)
                v.wait_ge(z_normed, 16 + 4 * t + 4)
                v.tensor_tensor(zt, zt, sgu_g[:].unsqueeze(1).broadcast_to([P, GROUPS, P]), ALU.mult).then_inc(z_step, 1)
            for t in range(TT):
                zt = big[:, 16 + t, :].rearrange("p (g i) -> p g i", g=GROUPS)
                v.wait_ge(z_step, 33 + t + 1)
                v.tensor_tensor(zt, zt, sgu_b[:].unsqueeze(1).broadcast_to([P, GROUPS, P]), ALU.add).then_inc(z_normed, 1)
            v.wait_ge(cond_ready, 1)
            for n in range(ADA_STEP):
                v.wait_ge(ada_landed[n % 4], 16 * (n // 4 + 1))
                dve_ada(v, n, n % 4, n)
            v.wait_ge(ada_done, ADA_STEP)
            v.tensor_copy(mods[:, 0:ADA_STEP], ada_part[:]).then_inc(ada_copied, 1)
            for g in range(GROUPS):
                v.wait_ge(mixed_ready, g + 1)
                v.tensor_tensor(tmp[:, g, :].rearrange("p (t i) -> p t i", t=TT), bank[5 + g % 3][:].rearrange("p (t i) -> p t i", t=TT),
                                bs[:, g, :].unsqueeze(1).broadcast_to([P, TT, P]), ALU.add).then_inc(mixed_step, 1)
                v.wait_ge(mixed_step, g + 1)
                if g == 0:
                    v.wait_ge(*freed("u", 4))
                v.tensor_tensor(big[:, 12 + g, :], big[:, 12 + g, :], tmp[:, g, :], ALU.mult).then_inc(sgu_ready, 1)
            for c in range(4):
                dve_add_square(v, "sgu", c)
            dve_var(v, "sgu", ATT)
            v.wait_ge(block_done, START["out1"])
            dve_scale_split(v, "sgu", "sgu", 4, lambda c: big[:, 12 + c, :], lambda c: vec("sgu_out_norm", c), first=4)
            v.wait_ge(bias_landed, 16)
            dve_attention(v, a_sems, a_units, lambda h, cols: bias[:, h, S - cols:S], 0)
            for c in range(4):
                dve_add_square(v, "attn", c)
            dve_var(v, "attn", ATT)
            dve_scale_split(v, "attn", "attn", 4, lambda c: big[:, c, :], lambda c: vec("attn_out_norm", c))
            dve_norm_x(v, "post_mix")
            dve_post_norm(v, "post_mix", 0)
            dve_norm_x(v, "pre_ffn")
            dve_scale_split(v, "pre_ffn", "pre_ffn", DC, lambda c: x[:, c, :], lambda c: vec("ln_pre_ffn", c))
            with v.Fori(0, FC // 2) as r:
                for jj in range(2):
                    v.wait_ge(silu_ready, jj + 1 + 2 * r)
                    v.wait_ge(block_done, START["gu1"] + 2 * jj + 2 + 4 * r)
                    v.tensor_tensor(big[:, bass.ds(r * 2 + jj, 1), :].rearrange("p o s -> p (o s)"), tmp[:, 2 * jj, :],
                                    bank[2 * jj + 1][:], ALU.mult).then_inc(banks_free["dve"], 2)
                    for m in range(4):
                        v.wait_ge(ada_landed[m], r * 32 + 16 * (3 + jj))
                        if jj == 0 and m == 0:
                            v.wait_ge(ada_copied, r + 1)
                        dve_ada(v, None, m, 4 * jj + m)
                v.wait_ge(ada_done, r * ADA_STEP + 2 * ADA_STEP)
                v.tensor_copy(mods[:, bass.ds(r * ADA_STEP + ADA_STEP, ADA_STEP)], ada_part[:]).then_inc(ada_copied, 1)
            v.wait_ge(ada_copied, 2 * MOD // ADA_STEP)
            v.tensor_tensor(mods[:], mods[:], vec("ada_b_2", 0, 2 * MOD), ALU.add).then_inc(mods_ready, 1)
            v.wait_ge(mods_ready, 1)
            for n in range(4):
                layer, which = n // 2, (1, 4)[n % 2]
                name = ("norm_mix_2", "norm_ffn_2")[n % 2]
                at = layer * MOD + which * DC
                v.scalar_tensor_tensor(gains[:, n, :], mods[:, at:at + DC], 1.0, vec(name, layer * DC, DC), ALU.add,
                                       ALU.mult).then_inc(mods_ready, 1)
            dve_split_hidden(v, "down1")
            for k in range(2):
                v.wait_ge(hi_ready, SPLIT_AT["p"] + k + 1)
                v.tensor_tensor(a_lo[:, 4 + k, :], big[:, 22 + k, :], f32(a_hi[:, 4 + k, :]), ALU.subtract).then_inc(lo_ready, 1)
            dve_norm_x(v, "post_ffn")
            dve_post_norm(v, "post_ffn", 1)
            for c in range(DC):
                v.wait_ge(hi_ready, SPLIT_AT["pe_gate"] + c + 1)
                v.tensor_tensor(a_lo[:, c, :], x[:, c, :], f32(a_hi[:, c, :]), ALU.subtract).then_inc(lo_ready, 1)
            for c in range(DC):
                v.wait_ge(*freed("pe_gate", c + 1))
                v.tensor_tensor(tmp[:, c % 4, :], tmp[:, c % 4, :], big[:, c, :], ALU.mult).then_inc(gate_step, 1)
                v.wait_ge(gate_step, c + 1)
                v.tensor_tensor(x[:, c, :], x[:, c, :], tmp[:, c % 4, :], ALU.add).then_inc(x_ready, 1)
            dve_norm_x(v, "mix0")
            v.wait_ge(mods_ready, 5)
            dve_scale_split(v, "mix0", "mix0", DC, lambda c: x[:, c, :], lambda c: gains[:, 0, c:c + 1], lambda c: mod(0, 0, c))
            dve_stick(v)
            for c in range(DC):
                v.wait_ge(hi_ready, SPLIT_AT["battn"] + c + 1)
                v.tensor_tensor(a_lo[:, c, :], big[:, 2 * c, :], f32(a_hi[:, c, :]), ALU.subtract).then_inc(lo_ready, 1)
            dve_residual(v, "out2", 0, 2, lambda c: v.wait_ge(block_done, START["out2"] + c + 1), 4)
            dve_norm_x(v, "ffn0")
            dve_scale_split(v, "ffn0", "ffn0", DC, lambda c: x[:, c, :], lambda c: gains[:, 1, c:c + 1], lambda c: mod(0, 3, c))
            dve_conv(v, 0)
            dve_split_hidden(v, "down2")
            dve_residual(v, "down2", 0, 5, lambda c: wait_down(v, 1, c), 8)
            dve_norm_x(v, "mix1")
            dve_scale_split(v, "mix1", "mix1", DC, lambda c: x[:, c, :], lambda c: gains[:, 2, c:c + 1], lambda c: mod(1, 0, c))
            v.wait_ge(wi_landed, 16)
            v.tensor_copy(wi_hi[:].rearrange("p k h -> p (k h)"), wi_raw[:]).then_inc(wi_split, 1)
            v.wait_ge(wi_split, 1)
            v.tensor_tensor(wi_lo[:].rearrange("p k h -> p (k h)"), wi_raw[:], f32(wi_hi[:]).rearrange("p k h -> p (k h)"),
                            ALU.subtract).then_inc(wi_split, 1)
            v.memset(tmp[64:P, 2, :], 0.0).then_inc(index_init, 1)
            v.memset(tmp[0:64, 3, :], 0.0).then_inc(index_init, 1)
            for i in range(1, TT):
                v.memset(big[:, 20 + i, 0:i * P], 0.0).then_inc(index_init, 1)
                v.tensor_copy(big[:, 20 + i, i * P:(i + 1) * P], causal).then_inc(index_init, 1)
            v.tensor_copy(not_selected[:, 0, 0:P], causal).then_inc(selected, 1)
            v.tensor_scalar(kq_gain[:], vec("dsa_k_norm_2", 0), vec("dsa_q_norm_2", 0), D_LAT ** -0.5, ALU.mult, ALU.mult).then_inc(lat_split, 1)

            def index_add(n):
                i, h = 1 + n // IDX_HEADS, n % IDX_HEADS
                cols = P * (i + 1)
                v.wait_ge(relu_ready, n + 1)
                if n == 0:
                    v.wait_ge(wi_taken, 1)
                    v.wait_ge(index_init, 8)
                else:
                    v.wait_ge(index_added, n)
                v.scalar_tensor_tensor(big[:, 20 + i, 0:cols], probs_t[:, n % 4, 0:cols], wi[:, i, h:h + 1], big[:, 20 + i, 0:cols],
                                       ALU.mult, ALU.add).then_inc(index_added, 1)

            def top_round(n):
                i, turn = 1 + n // (TOPK // 8), n % (TOPK // 8)
                cols = P * (i + 1)
                scores = big[:, 20 + i, 0:cols]
                if turn == 0:
                    v.wait_ge(index_added, i * IDX_HEADS)
                if n:
                    v.wait_ge(top_step, 2 * n)
                v.max(top8[:], scores).then_inc(top_step, 1)
                v.wait_ge(top_step, 2 * n + 1)
                v.match_replace(scores, top8[:], scores, TAKEN).then_inc(top_step, 1)
                if turn == TOPK // 8 - 1:
                    v.wait_ge(top_step, 2 * n + 2)
                    v.tensor_scalar(not_selected[:, i, 0:cols], scores, TAKEN, NEG, ALU.not_equal, ALU.mult).then_inc(selected, 1)

            rounds = [0, 0, 0, 4, 4, 4, 4] + [3] * 8 + [4] * 2
            assert sum(rounds) == 3 * (TOPK // 8)
            for m in range(D_HEADS + 1):
                v.wait_ge(qsum_ready, m + 1)
                if m:
                    v.wait_ge(qrstd_ready, m)
                v.tensor_scalar(var[:], sum_bank[:], 1.0 / D_LAT, EPS, ALU.mult, ALU.add).then_inc(qvar_ready, 1)
                v.wait_ge(qvar_ready, 2 * m + 1)
                v.reciprocal(var[:], var[:]).then_inc(qvar_ready, 1)
                if m == 0:
                    v.wait_ge(lat_split, 2)
                    v.tensor_tensor(lat_lo[:], bank[0][:], f32(lat_hi[:]), ALU.subtract).then_inc(lat_split, 1)
                for n in range(4 * m - 4, min(4 * m, 3 * IDX_HEADS)):
                    if n >= 0:
                        index_add(n)
                for n in range(sum(rounds[:m]), sum(rounds[:m + 1])):
                    top_round(n)
                v.wait_ge(qrstd_ready, m + 1)
                if m == 0:
                    v.scalar_tensor_tensor(k_lat[:], bank[0][:], kq_gain[:, 0:1], rstd[:], ALU.mult, ALU.mult).then_inc(banks_free["dve"], 1)
                else:
                    v.tensor_tensor(big[:, m - 1, :], bank[m % 4][:], rstd[:], ALU.mult).then_inc(banks_free["dve"], 1)
            v.wait_ge(tables_landed, 32)
            dve_attention(v, d_sems, d_units, lambda h, cols: (y if h < 8 else bias)[:, h % 8, cols - 1::-1], n_stat // 2,
                          low=lambda v, c: dve_low_of_bank(v, "dattn", c, bank[6 + c % 2]))
            dve_residual(v, "out3", 1, 2, lambda c: v.wait_ge(block_done, START["out3"] + c + 1), 4)
            dve_norm_x(v, "ffn1")
            dve_scale_split(v, "ffn1", "ffn1", DC, lambda c: x[:, c, :], lambda c: gains[:, 3, c:c + 1], lambda c: mod(1, 3, c))
            dve_conv(v, 1)
            dve_split_hidden(v, "down3")
            dve_residual(v, "down3", 1, 5, lambda c: wait_down(v, 2, c), 8)


def constant_tiles():
    i = np.arange(P)
    row, col = i[:, None], i[None, :]
    tiles = {"ident": row == col, "ones": np.ones((P, P)), "neg_ones": -np.ones((P, P)),
             "neg_suffix": np.where(row >= col, -1.0, 0.0), "upper": col >= row,
             "causal": np.where(col > row, NEG, 0.0), "strict": np.where(row >= col, NEG, 0.0)}
    return np.stack([np.asarray(tiles[n], np.float32) for n in CONSTS], axis=1)


def first_bias():
    p, m = np.arange(P)[:, None], np.arange(S)[None, :]
    dist = p - (m - (S - P))
    count = (dist <= 128) * 1 + (dist % 4 == 0) * 1 + (dist % 16 == 0) * 1
    valid = (dist >= 0) & (count > 0)
    slopes = 2.0 ** (-8.0 * (np.arange(A_HEADS) + 1.0) / A_HEADS)
    b = -slopes[None, :, None] * dist[:, None, :] + np.log(np.maximum(count, 1))[:, None, :]
    return np.where(valid[:, None, :], b, NEG).astype(np.float32)


def bucket_onehot():
    dist = np.maximum(np.arange(SPAN) - (P - 1), 0)
    exact = BUCKETS // 2
    nf = np.maximum(dist, 1).astype(np.float32)
    large = exact + (np.log(nf / np.float32(exact)) / np.float32(math.log(MAX_DIST / exact)) * (BUCKETS - exact)).astype(np.int32)
    bucket = np.where(dist < exact, dist, np.minimum(large, BUCKETS - 1))
    hot = (np.arange(BUCKETS)[:, None] == bucket[None, :]) & (np.arange(SPAN) >= P - 1)[None, :]
    return hot.astype(np.float32)


def tile_blocks(w):
    k, n = w.shape
    return w.reshape(k // P, P, n // P, P).transpose(2, 1, 0, 3).reshape(n // P, P, k)


def token_blocks(w):
    k, n = w.shape
    return w.reshape(k // 256, 2, P, n // S, S).transpose(3, 0, 2, 1, 4).reshape(-1, P, BLOCK)


def chunked(v):
    return v.reshape(-1, P).T


def pair_blocks(w):
    n = w.shape[1] // 2
    return np.stack([tile_blocks(w[:, :n]), tile_blocks(w[:, n:])], axis=1).reshape(-1, P, BLOCK)


def weight_stream(a):
    w_in, sb_in, dsa = a["w_in"][0], a["sb_w_in_2"][0], a["dsa_w_in_2"][0]
    o1 = D_HEADS * D_LAT
    o2 = o1 + D_LAT
    o3 = o2 + IDX_HEADS * IDX_DIM
    o4 = o3 + IDX_DIM
    ki = dsa[:, o3:o4]
    parts = {
        "q": tile_blocks(w_in[:, 0:ATT]), "k": tile_blocks(w_in[:, ATT:2 * ATT]), "v": token_blocks(w_in[:, 2 * ATT:3 * ATT]),
        "u": tile_blocks(w_in[:, 3 * ATT:4 * ATT]), "z": token_blocks(w_in[:, 4 * ATT:5 * ATT]),
        "out1": tile_blocks(a["w_out"][0]), "gu1": pair_blocks(a["w_gate_up"][0]), "down1": a["w_down"][0].reshape(FC, P, D),
        "pe_proj": a["w_pe_proj"][0].reshape(2, P, 2, 4, P).transpose(2, 1, 3, 0, 4).reshape(2, P, BLOCK),
        "pe_gate": tile_blocks(a["w_pe_gate"][0]),
        "bq": tile_blocks(sb_in[:, 0:D]), "bk": tile_blocks(sb_in[:, D:2 * D]), "bv": token_blocks(sb_in[:, 2 * D:3 * D]),
        "out2": tile_blocks(a["sb_w_out_2"][0]),
        "gu2": pair_blocks(a["ffn_w_up_2"][0]), "down2": a["ffn_w_down_2"][0].reshape(FC, P, D),
        "qi": tile_blocks(dsa[:, o2:o3]), "ki": tile_blocks(np.concatenate([ki, ki], axis=1)), "lat": tile_blocks(dsa[:, o1:o2]),
        "dq": tile_blocks(dsa[:, 0:o1]), "uv": a["dsa_w_uv_2"][0].transpose(1, 0, 2).reshape(1, P, BLOCK),
        "out3": tile_blocks(a["dsa_w_out_2"][0]),
        "gu3": pair_blocks(a["ffn_w_up_2"][1]), "down3": a["ffn_w_down_2"][1].reshape(FC, P, D),
    }
    return np.concatenate([parts[name] for name, _ in PHASES], axis=0)


def vectors(a):
    conv_w = a["ffn_conv_w_2"].reshape(2, 3, 2, FC, P)
    conv_b = a["ffn_conv_b_2"].reshape(2, 1, 2, FC, P)
    conv = np.concatenate([conv_w, conv_b], axis=1).transpose(4, 0, 3, 2, 1).reshape(P, -1)
    parts = [conv if name == "conv" else chunked(a[name]) for name, _ in VECS]
    return np.concatenate(parts, axis=1)


def feature_major(t, n):
    return t.reshape(S, n, P).transpose(2, 1, 0)


def kernel(**inputs):
    import concourse.bacc as bacc
    from concourse.bass_utils import run_bass_kernel_spmd

    a = {k: np.asarray(v) for k, v in inputs.items()}
    wi = a["dsa_w_in_2"][0][:, -IDX_HEADS:]
    arrays = {
        "x": feature_major(a["x"][0], DC),
        "p": feature_major(a["p"][0, 0], PLE // P),
        "vecs": vectors(a),
        "stream": weight_stream(a),
        "ada": a["ada_w_2"].reshape(2, D, MOD, P).transpose(0, 2, 3, 1).reshape(2 * MOD, P, D),
        "consts": constant_tiles(),
        "bias": first_bias(),
        "onehot": bucket_onehot(),
        "rel": a["rel_bias_2"],
        "wi": wi.reshape(DC, P, IDX_HEADS).transpose(1, 0, 2).reshape(P, DC * IDX_HEADS),
        "sgu_g": a["sgu_ln_g"][0],
        "sgu_b": a["sgu_ln_b"][0],
        "bs": a["b_spatial"][0].reshape(-1),
        "ws": a["w_spatial"][0].transpose(2, 0, 1),
        "c": a["c_2"][0],
    }
    arrays = {f"in_{k}": np.ascontiguousarray(v) for k, v in arrays.items()}
    nc = bacc.Bacc("TRN2", target_bir_lowering=False, num_devices=1)
    args = [nc.dram_tensor(k, v.shape, F32, kind="ExternalInput").ap() for k, v in arrays.items()]
    scratch = nc.dram_tensor("rel_rows", (D_HEADS, SPAN), F32, kind="Internal").ap()
    out = nc.dram_tensor("out", (P, DC, S), F32, kind="ExternalOutput").ap()
    two_blocks(nc, *args, scratch, out)
    r = run_bass_kernel_spmd(nc, [arrays], core_ids=[0])
    got = r.results[0]["out"]
    return got.transpose(2, 1, 0).reshape(1, S, D)
```

```python
from contextlib import ExitStack
import math

import numpy as np
import concourse.bass as bass
from concourse import mybir

F32 = mybir.dt.float32
F32R = mybir.dt.float32r
BF16 = mybir.dt.bfloat16
U32 = mybir.dt.uint32
ACT = mybir.ActivationFunctionType
ALU = mybir.AluOpType

P = 128
S = 512
D = 1024
DC = D // P
TT = S // P
ATT = 512
A_HEADS, A_HD = 8, 64
GROUPS = 4
FF = 2816
FC = FF // P
PLE = 256
B_HEADS, B_HD = 16, 64
D_HEADS, D_LAT, D_V = 16, 128, 64
IDX_HEADS, IDX_DIM = 8, 64
TOPK = 128
BUCKETS, MAX_DIST = 32, 128
EPS = 1e-6
NEG = -1e30
TAKEN = -3e38
BLOCK = D
RAW = 4
SPLIT = 2
X_PARTS = 4
MOD = 6 * DC
SPAN = 640
ADA_STEP = 8

PHASES = [("z", 4), ("u", 4), ("q", 4), ("k", 4), ("v", 4), ("out1", 8), ("gu1", 2 * FC), ("down1", FC),
          ("pe_proj", 2), ("pe_gate", 8),
          ("bq", 8), ("bk", 8), ("bv", 8), ("out2", 8), ("gu2", 2 * FC), ("down2", FC),
          ("qi", 4), ("ki", 1), ("lat", 1), ("dq", 16), ("uv", 1), ("out3", 8), ("gu3", 2 * FC), ("down3", FC)]
START, _n = {}, 0
for _name, _count in PHASES:
    START[_name] = _n
    _n += _count
N_BLOCKS = _n
COUNT = dict(PHASES)

TILES = [("z", "act", 4), ("u", "act", 4), ("q", "act", 4), ("k", "act", 4), ("v", "act", 4), ("out1", "act", 8),
         ("gu1", "dve", 44), ("pe_proj", "act", 8), ("pe_gate", "act", 8), ("bq", "act", 8), ("bk", "act", 8),
         ("bv", "act", 8), ("out2", "x", 8), ("gu2", "dve", 44), ("qi", "act", 4), ("ki", "act", 1),
         ("lat", "act", 1), ("dq", "act", 16), ("uv", "act", 8), ("out3", "x", 8), ("gu3", "dve", 44)]
FREED, _t = {}, {"act": 0, "dve": 0, "x": 0}
for _name, _eng, _count in TILES:
    FREED[_name] = (_eng, dict(_t))
    _t[_eng] += _count
FREED["end"] = ("act", dict(_t))

SPLITS = [("pre_mix", 8), ("sgu", 4), ("attn", 4), ("pre_ffn", 8), ("down1", FC), ("p", 2), ("pe_gate", 8), ("mix0", 8),
          ("battn", 8), ("ffn0", 8), ("down2", FC), ("mix1", 8), ("dattn", 8), ("ffn1", 8), ("down3", FC)]
SPLIT_AT, _n = {}, 0
for _name, _count in SPLITS:
    SPLIT_AT[_name] = _n
    _n += _count

POOL_LOWS = ["pre_mix", "pre_ffn", "mix0", "ffn0", "mix1", "ffn1"]
POOL_AT = {name: DC // 2 * n for n, name in enumerate(POOL_LOWS)}
LOW_AT, _n = {}, 0
for _name, _count in SPLITS:
    LOW_AT[_name] = _n
    _n += _count // 2 if _name in POOL_LOWS else _count

NORM_GROUPS = {"pre_mix": (8,), "sgu": (4,), "attn": (3, 1), "post_mix": (7, 1), "pre_ffn": (2, 2, 2, 1, 1),
               "post_ffn": (2, 2, 2, 1, 1), "mix0": (7, 1), "ffn0": (7, 1), "mix1": (2, 2, 2, 1, 1), "ffn1": (7, 1)}
NORM_INDEX = {name: n for n, name in enumerate(NORM_GROUPS)}
NORM_CHUNKS = {name: sum(groups) for name, groups in NORM_GROUPS.items()}
SQUARE_AT, GROUP_AT, ADDED_AT, _k, _g = {}, {}, {}, 0, 0
for _name, _groups in NORM_GROUPS.items():
    SQUARE_AT[_name], GROUP_AT[_name], ADDED_AT[_name] = _k, _g, _k - _g
    _k, _g = _k + sum(_groups), _g + len(_groups)


def square_place(name, c):
    before = 0
    for g, size in enumerate(NORM_GROUPS[name]):
        if c < before + size:
            return g, c - before, ADDED_AT[name] + c - g - 1
        before += size


X_AT = {"post_mix": 0, "post_ffn": 8, "pe_gate": 16, "out2": 24, "down2": 32, "out3": 40, "down3": 48}
T_AT = {"pre_mix": 0, "sgu": 8, "attn": 12, "pre_ffn": 16, "mix0": 24, "ffn0": 32, "mix1": 40, "ffn1": 48}

VECS = [("ln_pre_mix", 8), ("attn_out_norm", 4), ("sgu_out_norm", 4), ("ln_post_mix", 8), ("ln_pre_ffn", 8),
        ("ln_post_ffn", 8), ("b_pe_gate", 8), ("norm_mix_2", 16), ("norm_ffn_2", 16), ("ada_b_2", 2 * MOD),
        ("dsa_q_norm_2", 1), ("dsa_k_norm_2", 1), ("conv", 2 * FC * 8)]
VEC, _n = {}, 0
for _name, _count in VECS:
    VEC[_name] = _n
    _n += _count
N_VECS = _n
CONSTS = ["ident", "ones", "neg_ones", "neg_suffix", "upper", "causal", "strict"]


def two_blocks(nc, x_in, p_in, vecs_in, stream_in, ada_in, consts_in, bias_in, onehot_in, rel_in, wi_in,
               sgu_g_in, sgu_b_in, bs_in, ws_in, c_in, scratch, out):
    ctx = ExitStack()

    def sb(name, shape, dt=F32, stack=None):
        return (stack or ctx).enter_context(nc.sbuf_tensor(name, shape, dt))

    def sem(name):
        return ctx.enter_context(nc.semaphore(name))

    with ctx:
        x = sb("x", [P, DC, S])
        a_hi = sb("a_hi", [P, DC, S], F32R)
        a_lo = sb("a_lo", [P, DC, S], F32R)
        raw = sb("raw", [P, RAW, BLOCK])
        w_hi = sb("w_hi", [P, SPLIT, BLOCK], F32R)
        w_lo = sb("w_lo", [P, SPLIT, BLOCK], F32R)
        big = sb("big", [P, 24, S])
        tmp = sb("tmp", [P, 4, S])
        y = sb("y", [P, DC, S])
        bias = sb("bias", [P, DC, S])
        squares = sb("squares", [P, 2, S])
        square_sum = sb("square_sum", [P, 2, S])
        diag = sb("diag", [P, TT, P])
        rms = sb("rms", [P, 5, TT])
        vecs = sb("vecs", [P, N_VECS])
        consts = sb("consts", [P, len(CONSTS), P])
        ident_b = sb("ident_b", [P, P], BF16)
        strict_b = sb("strict_b", [P, P], BF16)
        neg_ones_r = sb("neg_ones_r", [P, P], F32R)
        neg_suffix_r = sb("neg_suffix_r", [P, P], F32R)
        mods = sb("mods", [P, 2 * MOD])
        gains = sb("gains", [P, 4, DC])
        kq_gain = sb("kq_gain", [P, 1])
        ada_part = sb("ada_part", [P, ADA_STEP])
        n_stat = 2 * D_HEADS * TT
        neg_max = sb("neg_max", [P, n_stat])
        den = sb("den", [P, n_stat])
        rden = sb("rden", [P, n_stat])
        z_stat = sb("z_stat", [P, 16, 6])
        z_mv = sb("z_mv", [P, 16, 2])
        z_rstd = sb("z_rstd", [P, 16])
        wi_raw = sb("wi_raw", [P, DC * IDX_HEADS])
        wi_hi = sb("wi_hi", [P, DC, IDX_HEADS], F32R)
        wi_lo = sb("wi_lo", [P, DC, IDX_HEADS], F32R)
        wi = sb("wi", [P, TT, IDX_HEADS])
        top8 = sb("top8", [P, 8])
        with ExitStack() as first:
            sgu_g = sb("sgu_g", [P, P], F32, first)
            sgu_b = sb("sgu_b", [P, P], F32, first)
            bs = sb("bs", [P, GROUPS, P], F32, first)
            ws = sb("ws", [P, GROUPS, P], F32, first)
        with ExitStack() as second:
            probs_t = sb("probs_t", [P, 4, S], F32, second)
            ctx.push(second.pop_all())
        with ExitStack() as first:
            cond = sb("cond", [P, D], F32, first)
        with ExitStack() as second:
            k_lat = sb("k_lat", [P, S], F32, second)
            not_selected = sb("not_selected", [P, TT, S], BF16, second)
            lat_hi = sb("lat_hi", [P, S], F32R, second)
            lat_lo = sb("lat_lo", [P, S], F32R, second)
            ctx.push(second.pop_all())

        bank = [ctx.enter_context(nc.psum_tensor(f"bank{i}", [P, S], F32)) for i in range(8)]
        rstd_bank = bank[5]

        ident = consts[:, 0, :]
        ones = consts[:, 1, :]
        neg_ones = consts[:, 2, :]
        neg_suffix = consts[:, 3, :]
        upper = consts[:, 4, :]
        causal = consts[:, 5, :]
        strict = consts[:, 6, :]

        q_rms = squares[:, 0, 0:5 * D_HEADS * TT].rearrange("p (k n) -> p k n", k=5)

        def vec(name, c, n=1):
            return vecs[:, VEC[name] + c:VEC[name] + c + n]

        def mod(layer, which, c):
            return mods[:, layer * MOD + which * DC + c:layer * MOD + which * DC + c + 1]

        def f32(ap):
            return ap.bitcast(F32)

        raw_landed = [sem(f"raw_landed{j}") for j in range(RAW)]
        zeroed = sem("zeroed")
        split_begun = sem("split_begun")
        high_ready = sem("high_ready")
        split_ready = sem("split_ready")
        block_done = sem("block_done")
        banks_free = {"act": sem("banks_free_act"), "dve": sem("banks_free_dve")}
        down_done = sem("down_done")
        down_taken = sem("down_taken")
        vecs_landed, consts_landed, bias_landed = sem("vecs_landed"), sem("consts_landed"), sem("bias_landed")
        x_landed = [sem(f"x_landed{j}") for j in range(X_PARTS)]
        rows_landed, cond_landed, p_landed, wi_landed = sem("rows_landed"), sem("cond_landed"), sem("p_landed"), sem("wi_landed")
        onehot_landed = sem("onehot_landed")
        masks_ready = sem("masks_ready")
        sq_ready, sq_added, group_used = sem("sq_ready"), sem("sq_added"), sem("group_used")
        rms_ready, inverse_step, diag_ready, rstd_ready = sem("rms_ready"), sem("inverse_step"), sem("diag_ready"), sem("rstd_ready")
        scaled_ready, hi_ready, lo_ready, lo_pool_ready = sem("scaled_ready"), sem("hi_ready"), sem("lo_ready"), sem("lo_pool_ready")
        x_ready = sem("x_ready")
        z_step, z_std, z_normed = sem("z_step"), sem("z_std"), sem("z_normed")
        ws_masked = sem("ws_masked")
        mixed_ready, mixed_step, sgu_ready = sem("mixed_ready"), sem("mixed_step"), sem("sgu_ready")
        post_step = sem("post_step")
        silu_ready, conv_base, conv_step, hidden_ready = sem("silu_ready"), sem("conv_base"), sem("conv_step"), sem("hidden_ready")
        cond_ready, ada_done, ada_copied, mods_ready = sem("cond_ready"), sem("ada_done"), sem("ada_copied"), sem("mods_ready")
        ada_landed = [sem(f"ada_landed{j}") for j in range(4)]
        pe_ready, gate_ready, gate_step = sem("pe_ready"), sem("gate_ready"), sem("gate_step")
        index_init = sem("index_init")
        rel_row, rel_copied, rel_stored, tables_landed = sem("rel_row"), sem("rel_copied"), sem("rel_stored"), sem("tables_landed")
        out_stored = sem("out_stored")

        wi_split, wi_ready, wi_taken = sem("wi_split"), sem("wi_ready"), sem("wi_taken")
        relu_ready, index_ready, index_added = sem("relu_ready"), sem("index_ready"), sem("index_added")
        qsq_ready, qsum_ready, qrms_ready = sem("qsq_ready"), sem("qsum_ready"), sem("qrms_ready")
        k_diag_ready, k_rstd_ready, k_scaled = sem("k_diag_ready"), sem("k_rstd_ready"), sem("k_scaled")
        lat_split, uv_ready, selected, top_step = sem("lat_split"), sem("uv_ready"), sem("selected"), sem("top_step")

        def freed(name, n):
            eng, before = FREED[name]
            if eng == "x":
                return x_ready, X_AT[name] + n
            return banks_free[eng], 4 + before[eng] + n

        def low_done(name, c):
            if name not in POOL_LOWS:
                return lo_ready, LOW_AT[name] + c + 1
            return (lo_pool_ready, POOL_AT[name] + c // 2 + 1) if c % 2 else (lo_ready, LOW_AT[name] + c // 2 + 1)

        def pe_begin(pe, name):
            before = FREED[name][1]
            pe.wait_ge(banks_free["act"], 4 + before["act"])
            pe.wait_ge(banks_free["dve"], 4 + before["dve"])

        def pe_three_passes(pe, o, lhs_hi, lhs_lo, rhs_hi, rhs_lo, start, stop, **kw):
            pe.matmul(o, lhs_hi, rhs_hi, start=start, stop=False, **kw)
            pe.matmul(o, lhs_hi, rhs_lo, start=False, stop=False, **kw)
            return pe.matmul(o, lhs_lo, rhs_hi, start=False, stop=stop, **kw)

        def pe_tile(pe, name, j, i, split=None, first_bank=0, norm=None):
            s = (START[name] + j) % SPLIT
            pe.wait_ge(split_ready, START[name] + 1 + i)
            counter, value = freed(name, i - 3)
            pe.wait_ge(counter, value)
            order = (4, 5, 6, 7, 0, 1, 2, 3) if name == "out1" else range(DC)
            for n, k in enumerate(order):
                if split == "attn" and n == 4:
                    pe_spread(pe, "attn")
                if split == "attn":
                    pe.wait_ge(*low_done("sgu" if n < 4 else "attn", n % 4))
                elif split is not None:
                    pe.wait_ge(*low_done(split, n))
                if norm and n == DC - 2:
                    pe_sum_group(pe, norm, 0)
                m = pe_three_passes(pe, bank[(j + first_bank) % 4][:], w_hi[:, s, k * P:(k + 1) * P], w_lo[:, s, k * P:(k + 1) * P],
                                    a_hi[:, k, :], a_lo[:, k, :], n == 0, n == DC - 1)
            m.then_inc(block_done, 1)

        def pe_tiles(pe, name, split=None, norm=None):
            n = COUNT[name]
            pe_begin(pe, name)
            if split is not None:
                for j in range(4):
                    pe_tile(pe, name, j, j, split if j == 0 else None)
            done = 4 if split is not None else 0
            if (n - done) // 4 > 1:
                with pe.Fori(done // 4, n // 4) as r:
                    for j in range(4):
                        pe_tile(pe, name, j, r * 4 + j)
                done = n // 4 * 4
            for i in range(done, n):
                pe_tile(pe, name, i % 4, i, norm=norm if i == n - 1 else None)

        def pe_token_tiles(pe, name, halves=1):
            pe_begin(pe, name)
            for h in range(halves):
                for b in range(4):
                    i = 4 * h + b
                    s = (START[name] + i) % SPLIT
                    pe.wait_ge(split_ready, START[name] + i + 1)
                    for t in range(TT):
                        if h and b == 0:
                            pe.wait_ge(*freed(name, t + 1))
                        for k2 in range(2):
                            k = 2 * b + k2
                            hi, lo = w_hi[:, s, k2 * S:(k2 + 1) * S], w_lo[:, s, k2 * S:(k2 + 1) * S]
                            xh, xl = a_hi[:, k, t * P:(t + 1) * P], a_lo[:, k, t * P:(t + 1) * P]
                            if name == "z" and t == 0:
                                pe.wait_ge(*low_done("pre_mix", k))
                            m = pe_three_passes(pe, bank[t][:], xh, xl, hi, lo, k == 0, k == DC - 1)
                    m.then_inc(block_done, 1)

        def sum_columns(name):
            return (bank[0] if name in ("post_ffn", "mix1") else bank[4])[:, 0:TT]

        def pe_sum_group(pe, name, g):
            size, before = NORM_GROUPS[name][g], sum(NORM_GROUPS[name][:g])
            if size > 1:
                pe.wait_ge(sq_added, ADDED_AT[name] + before + size - g - 1)
            else:
                pe.wait_ge(sq_ready, SQUARE_AT[name] + before + 1)
            for t in range(TT):
                m = pe.matmul(sum_columns(name)[:, t:t + 1], square_sum[:, (GROUP_AT[name] + g) % 2, t * P:(t + 1) * P], ones[:, 0:1],
                              start=g == t == 0, stop=g == len(NORM_GROUPS[name]) - 1, skip_group_check=True)
            m.then_inc(group_used, 1)

        def pe_spread(pe, name):
            pe.wait_ge(diag_ready, NORM_INDEX[name] + 1)
            pe.matmul(rstd_bank[:], ones, diag[:].rearrange("p t i -> p (t i)"), start=True, stop=True).then_inc(rstd_ready, 1)

        def pe_norm(pe, name, first=0):
            for g in range(first, len(NORM_GROUPS[name])):
                pe_sum_group(pe, name, g)
            pe_spread(pe, name)

        def pe_down(pe, name, n, norm=None):
            def chunk(j, i, start=False, stop=False):
                hi, lo = (first_hi, first_lo) if start else (a_hi[:, j, :], a_lo[:, j, :])
                s = (START[name] + j) % SPLIT
                pe.wait_ge(split_ready, START[name] + 1 + i)
                pe.wait_ge(lo_ready, LOW_AT[name] + 1 + i)
                for c in (4, 5, 6, 7, 0, 1, 2, 3) if start else range(DC):
                    if start and c == 0:
                        pe_begin(pe, {"down1": "pe_proj", "down2": "qi", "down3": "end"}[name])
                    m = pe_three_passes(pe, bank[c][:], w_hi[:, s, c * P:(c + 1) * P], w_lo[:, s, c * P:(c + 1) * P],
                                        hi, lo, start, stop, skip_group_check=True)
                    if stop and c < DC - 1:
                        m.then_inc(down_done, 1)
                    elif c == (3 if start else DC - 1):
                        m.then_inc(block_done, 1)
                    if stop and norm and c in (5, 7):
                        pe_sum_group(pe, norm, c // 2 - 2)
            for j in range(4):
                chunk(j, j, start=j == 0)
            with pe.Fori(1, FC // 4) as r:
                for j in range(4):
                    chunk(j, r * 4 + j)
            for i in range(FC // 4 * 4, FC):
                chunk(i % 4, i, stop=i == FC - 1)

        def attention(name, heads):
            sems = {k: sem(f"{name}_{k}") for k in
                    ("scores", "scaled", "masked", "exp", "rden", "normed", "turned", "copied", "out", "evac")}
            units = [(h, i) for h in range(heads) for i in range(TT)]
            return sems, units

        a_sems, a_units = attention("a", A_HEADS)
        d_sems, d_units = attention("d", D_HEADS)

        head_sums = bank[7][:, TT * IDX_HEADS:TT * IDX_HEADS + (D_HEADS + 1) * TT]

        def out_bank(h):
            return bank[6 + (h // 2) % 2]

        def pe_attention(pe, sems, units, queries, keys, values, probs, mask, evacuated, read="masked"):
            n = len(units)
            for step in range(n + 4):
                if step < n:
                    h, i = units[step]
                    cols = P * (i + 1)
                    if step >= 3:
                        pe.wait_ge(sems[read], step - 2)
                    b = bank[step % 3]
                    m = pe.matmul(b[:, 0:cols], queries(h, i), keys(h, cols), start=True, stop=mask is None)
                    if mask is not None:
                        m = pe.matmul(b[:, 0:cols], ident_b[:], mask(i, cols), start=False, stop=True)
                    m.then_inc(sems["scores"], 1)
                if 3 <= step < n + 3:
                    u = step - 3
                    h, i = units[u]
                    pe.wait_ge(sems["normed"], u + 1)
                    if u >= 2:
                        pe.wait_ge(sems["copied"], u - 1)
                    for j in range(i + 1):
                        m = pe.transpose(bank[(3, 5)[u % 2]][:, j * P:(j + 1) * P], tmp[:, u % 4, j * P:(j + 1) * P], ident)
                    m.then_inc(sems["turned"], 1)
                if step >= 4:
                    u = step - 4
                    h, i = units[u]
                    pe.wait_ge(sems["copied"], u + 1)
                    if h >= 4 and h % 2 == 0 and i == 0:
                        pe.wait_ge(*evacuated(h // 2 - 2))
                    o = out_bank(h)[64 * (h % 2):64 * (h % 2) + 64, i * P:(i + 1) * P]
                    for j in range(i + 1):
                        m = pe.matmul(o, values(h, j), probs(u)[:, j * P:(j + 1) * P], start=j == 0, stop=j == i)
                    m.then_inc(sems["out"], 1)

        def dve_attention(v, sems, units, tables, base, low=None, scaled=False):
            for step in range(len(units) + 5):
                if low is not None and step >= 5 and units[step - 5][0] % 2 and units[step - 5][1] == TT - 1:
                    low(v, units[step - 5][0] // 2)
                if step < len(units):
                    u = step
                    h, i = units[u]
                    cols = P * (i + 1)
                    v.wait_ge(sems["scaled" if scaled else "scores"], u + 1)
                    if u >= 4 and not scaled:
                        v.wait_ge(sems["turned"], u - 3)
                    v.tensor_tensor_reduce(tmp[:, u % 4, 0:cols], (tmp[:, u % 4, :] if scaled else bank[u % 3])[:, 0:cols], tables(h, cols),
                                           -1.0, 3e38, ALU.add, ALU.min, neg_max[:, base + u:base + u + 1]).then_inc(sems["masked"], 1)
                if 1 <= step <= len(units):
                    u = step - 1
                    h, i = units[u]
                    cols = P * (i + 1)
                    v.wait_ge(sems["exp"], u + 1)
                    v.reciprocal(rden[:, base + u:base + u + 1], den[:, base + u:base + u + 1]).then_inc(sems["rden"], 1)
                    v.wait_ge(sems["rden"], u + 1)
                    v.tensor_scalar(tmp[:, u % 4, 0:cols], tmp[:, u % 4, 0:cols], rden[:, base + u:base + u + 1], None,
                                    ALU.mult).then_inc(sems["normed"], 1)

        def act_attention(a, sems, units, probs, base, evacuate, scale=None):
            late = scale is not None
            for step in range(len(units) + 3 + late):
                if late and step < len(units):
                    u = step
                    h, i = units[u]
                    cols = P * (i + 1)
                    a.wait_ge(sems["scores"], u + 1)
                    if u >= 4:
                        a.wait_ge(sems["turned"], u - 3)
                    a.activation(tmp[:, u % 4, 0:cols], bank[u % 3][:, 0:cols], ACT.Copy, scale=scale(h, i)).then_inc(sems["scaled"], 1)
                if late <= step < len(units) + late:
                    u = step - late
                    h, i = units[u]
                    cols = P * (i + 1)
                    a.wait_ge(sems["masked"], u + 1)
                    a.activation(tmp[:, u % 4, 0:cols], tmp[:, u % 4, 0:cols], ACT.Exp, bias=neg_max[:, base + u:base + u + 1],
                                 scale=-1.0, accum_out=den[:, base + u:base + u + 1]).then_inc(sems["exp"], 1)
                if 1 + late <= step <= len(units) + late:
                    u = step - 1 - late
                    h, i = units[u]
                    cols = P * (i + 1)
                    a.wait_ge(sems["turned"], u + 1)
                    if u >= 4:
                        a.wait_ge(sems["out"], u - 3)
                    a.activation(probs(u)[:, 0:cols], bank[(3, 5)[u % 2]][:, 0:cols], ACT.Copy).then_inc(sems["copied"], 1)
                if step >= 3 + late:
                    u = step - 3 - late
                    h, i = units[u]
                    if h % 2 and i == TT - 1:
                        a.wait_ge(sems["out"], u + 1)
                        evacuate(a, h // 2)

        b_z, b_neg, b_exp, b_ln, b_sp, b_hi, b_lo, b_e, b_a, b_out, b_evac = (
            sem(f"b_{k}") for k in ("scores", "neg_abs", "exp", "ln", "softplus", "high", "low", "logits", "weights", "out", "evac"))
        B_PLACE = [(0, 0), (1, 0), (2, 0), (1, 384)]
        B_COLS = [S, S, 256]
        B_ORDER = (1, 2, 0)
        B_TILES = {1: (1, 3), 2: (2,), 0: (0,)}
        y_flat = y[:].rearrange("p c s -> p (c s)")
        bias_flat = bias[:].rearrange("p c s -> p (c s)")
        hi_flat = a_hi[:].rearrange("p c s -> p (c s)")
        lo_flat = a_lo[:].rearrange("p c s -> p (c s)")

        def b_bank(h, n):
            return bank[(1, 5, 7)[h % 3] if n == 1 else ((0, 2), (3, 6))[h % 2][n // 2]]

        def b_slice(flat, slots, h, n, cols=None, at=0):
            o = (h % slots) * 1280 + n * S + at
            return flat[:, o:o + (B_COLS[n] if cols is None else cols)]

        def soft_buf(h, n):
            return b_slice(y_flat, 3, h, n)

        def sp_high(h, n, cols=None, at=0):
            return b_slice(hi_flat, 2, h, n, cols, at)

        def sp_low(h, n, cols=None, at=0):
            return b_slice(lo_flat, 2, h, n, cols, at)

        def weight_buf(h, n, cols=None, at=0):
            return b_slice(bias_flat, 3, h, n, cols, at)

        def b_values(h, j):
            return (tmp, probs_t)[h // 8][:, j, P * (h % 8 // 2):P * (h % 8 // 2) + P]

        def pe_stick(pe):
            for step in range(B_HEADS + 2):
                if step < B_HEADS:
                    h = step
                    for n in B_ORDER:
                        turns = 3 if n == 1 else 2
                        if h >= turns:
                            pe.wait_ge(b_a, 3 * (h - turns) + B_ORDER.index(n) + 1)
                        for j in B_TILES[n]:
                            at = B_PLACE[j][1]
                            w = S - P * j
                            pe.matmul(b_bank(h, n)[:, at:at + w], big[:, 16 + h // 2, j * P:(j + 1) * P],
                                      big[:, h, j * P:S], start=j != 3, stop=True, skip_group_check=True)
                            m = pe.matmul(b_bank(h, n)[:, at:at + P], ident_b[:], strict_b[:], start=False, stop=True,
                                          skip_group_check=True)
                        m.then_inc(b_z, 1)
                if 1 <= step <= B_HEADS:
                    h = step - 1
                    for n in B_ORDER:
                        pe.wait_ge(b_lo, 3 * h + (3 if n == 0 else 2))
                        for j in B_TILES[n]:
                            at = B_PLACE[j][1]
                            for j2 in range(j, TT):
                                n2, at2 = B_PLACE[j2]
                                w = S - P * j2
                                for part in (sp_high, sp_low):
                                    m = pe.matmul(b_bank(h, n)[:, at + P * (j2 - j):at + P * (j2 - j) + w],
                                                  (neg_suffix_r if j2 == j else neg_ones_r)[:], part(h, n2, w, at2),
                                                  start=False, stop=True, skip_group_check=True)
                        m.then_inc(b_e, 1)
                if step >= 2:
                    h = step - 2
                    pe.wait_ge(b_a, 3 * (h + 1))
                    if h:
                        pe.wait_ge(b_evac, h)
                    o = bank[4]
                    for j in range(TT):
                        n, at = B_PLACE[j]
                        w = S - P * j
                        m = pe.matmul(o[:, P * j:S], b_values(h, j), weight_buf(h, n, w, at), start=j == 0, stop=j == TT - 1)
                    m.then_inc(b_out, 1)

        def dve_stick(v):
            for h in range(B_HEADS):
                for k, n in enumerate(B_ORDER):
                    v.wait_ge(b_z, 3 * h + k + 1)
                    if h >= 3 and k == 0:
                        v.wait_ge(b_lo, 3 * (h - 2))
                    v.tensor_scalar(soft_buf(h, n).bitcast(U32), b_bank(h, n)[:, 0:B_COLS[n]].bitcast(U32), 0x80000000, None,
                                    ALU.bitwise_or).then_inc(b_neg, 1)
                for k, n in enumerate(B_ORDER):
                    v.wait_ge(b_ln, 3 * h + k + 1)
                    v.scalar_tensor_tensor(soft_buf(h, n), b_bank(h, n)[:, 0:B_COLS[n]], 0.0, soft_buf(h, n),
                                           ALU.max, ALU.add).then_inc(b_sp, 1)
                    if h >= 2 and k == 0:
                        v.wait_ge(b_e, 3 * (h - 1))
                    v.wait_ge(b_sp, 3 * h + k + 1)
                    v.tensor_copy(sp_high(h, n), soft_buf(h, n)).then_inc(b_hi, 1)

        def dve_low_of_bank(v, name, c, b):
            v.wait_ge(hi_ready, SPLIT_AT[name] + c + 1)
            v.tensor_tensor(a_lo[:, c, :], b[:], f32(a_hi[:, c, :]), ALU.subtract).then_inc(lo_ready, 1)

        def act_stick(a):
            for step in range(B_HEADS + 2):
                if step < B_HEADS:
                    h = step
                    for k, n in enumerate(B_ORDER):
                        a.wait_ge(b_neg, 3 * h + k + 1)
                        a.activation(soft_buf(h, n), soft_buf(h, n), ACT.Exp).then_inc(b_exp, 1)
                    for k, n in enumerate(B_ORDER):
                        a.wait_ge(b_exp, 3 * h + k + 1)
                        a.activation(soft_buf(h, n), soft_buf(h, n), ACT.Ln, bias=1.0).then_inc(b_ln, 1)
                if 1 <= step <= B_HEADS:
                    h = step - 1
                    for k, n in enumerate(B_ORDER):
                        a.wait_ge(b_e, 3 * h + k + 1)
                        if h >= 3 and k == 0:
                            a.wait_ge(b_out, h - 2)
                        a.activation(weight_buf(h, n), b_bank(h, n)[:, 0:B_COLS[n]], ACT.Exp).then_inc(b_a, 1)
                if step >= 2:
                    h = step - 2
                    rows = slice(64 * (h % 2), 64 * (h % 2) + 64)
                    a.wait_ge(b_out, h + 1)
                    a.activation(big[rows, h - h % 2, :], bank[4][rows, :], ACT.Copy).then_inc(b_evac, 1)

        def act_squares(a, name, srcs, waits):
            for c, src in enumerate(srcs):
                a.wait_ge(*waits(c))
                act_square(a, name, c, src)

        def act_square(a, name, c, src):
            g, place, added = square_place(name, c)
            g += GROUP_AT[name]
            if place == 0:
                if g >= 2:
                    a.wait_ge(group_used, g - 1)
                dst = square_sum[:, g % 2, :]
            else:
                if added >= 2:
                    a.wait_ge(sq_added, added - 1)
                dst = squares[:, added % 2, :]
            a.activation(dst, src, ACT.Square).then_inc(sq_ready, 1)

        def inverse_index(name):
            return NORM_INDEX[name] + 2 * (name == "ffn1")

        def act_rms(a, name):
            a.wait_ge(inverse_step, 5 * inverse_index(name) + 1)
            a.activation(rms[:, 0, :], rms[:, 1, :], ACT.Sqrt).then_inc(rms_ready, 1)

        def dve_inverse(v, steps, sums, width, rms_done, n):
            mean, r, a, b = (steps[:, k, :] for k in range(1, 5))
            v.tensor_scalar(mean, sums, 1.0 / width, EPS, ALU.mult, ALU.add).then_inc(inverse_step, 1)
            v.wait_ge(*rms_done)
            v.reciprocal(r, steps[:, 0, :]).then_inc(inverse_step, 1)
            v.wait_ge(inverse_step, 5 * n + 2)
            v.scalar_tensor_tensor(a, r, -0.5, mean, ALU.mult, ALU.mult).then_inc(inverse_step, 1)
            v.wait_ge(inverse_step, 5 * n + 3)
            v.tensor_tensor(b, a, r, ALU.mult).then_inc(inverse_step, 1)
            v.wait_ge(inverse_step, 5 * n + 4)
            v.scalar_tensor_tensor(mean, b, 1.5, r, ALU.add, ALU.mult).then_inc(inverse_step, 1)
            v.wait_ge(inverse_step, 5 * n + 5)

        def dve_diag(v, name, add=True, wait=True):
            s = NORM_INDEX[name]
            if add:
                dve_add_squares(v, name)
            v.wait_ge(group_used, GROUP_AT[name] + len(NORM_GROUPS[name]))
            dve_inverse(v, rms, sum_columns(name), P * NORM_CHUNKS[name], (rms_ready, s + 1), inverse_index(name))
            dve_write_diag(v).then_inc(diag_ready, 1)
            if wait:
                v.wait_ge(rstd_ready, s + 1)

        def dve_add_square(v, name, c):
            g, place, added = square_place(name, c)
            if place:
                v.wait_ge(sq_ready, SQUARE_AT[name] + c + 1)
                if place > 1:
                    v.wait_ge(sq_added, added)
                group = square_sum[:, (GROUP_AT[name] + g) % 2, :]
                v.tensor_tensor(group, group, squares[:, added % 2, :], ALU.add).then_inc(sq_added, 1)

        def dve_add_squares(v, name):
            for c in range(NORM_CHUNKS[name]):
                dve_add_square(v, name, c)

        def dve_write_diag(v):
            return v.tensor_tensor(diag[:], ident.unsqueeze(1).broadcast_to([P, TT, P]),
                                   rms[:, 1, :].unsqueeze(2).broadcast_to([P, TT, P]), ALU.mult)

        def write_low(e, sem_done, split, c, shift=None, first=0):
            e.wait_ge(hi_ready, SPLIT_AT[split] + c + 1)
            hi, lo = f32(a_hi[:, first + c, :]), a_lo[:, first + c, :]
            if shift is None:
                e.tensor_tensor(lo, tmp[:, c % 4, :], hi, ALU.subtract).then_inc(sem_done, 1)
            else:
                e.scalar_tensor_tensor(lo, tmp[:, c % 4, :], shift(c), hi, ALU.add, ALU.subtract).then_inc(sem_done, 1)

        def dve_scale_split(v, name, split, chunks, srcs, gain, shift=None, first=0):
            shared = split in POOL_LOWS
            for c in range(chunks + 1):
                if c < chunks:
                    if shared and c in (5, 7):
                        v.wait_ge(*low_done(split, c - 4))
                    v.scalar_tensor_tensor(tmp[:, c % 4, :], srcs(c), gain(c), rstd_bank[:], ALU.mult, ALU.mult).then_inc(scaled_ready, 1)
                if c >= 1 and not (shared and c % 2 == 0):
                    write_low(v, lo_ready, split, c - 1, shift, first)

        def act_high(a, name, chunks, shift=None, first=0):
            for c in range(chunks):
                a.wait_ge(scaled_ready, T_AT[name] + c + 1)
                if shift is None:
                    a.activation(a_hi[:, first + c, :], tmp[:, c % 4, :], ACT.Copy).then_inc(hi_ready, 1)
                elif c % 2 == 0:
                    a.activation(a_hi[:, first + c, :], tmp[:, c % 4, :], ACT.Identity, bias=shift(c)).then_inc(hi_ready, 1)
                else:
                    a.activation(a_hi[:, first + c, :], tmp[:, c % 4, :], ACT.Identity, bias=shift(c))
                    a.activation(tmp[:, c % 4, :], tmp[:, c % 4, :], ACT.Identity, bias=shift(c)).then_inc(hi_ready, 1)

        first_hi, first_lo = lat_hi[:], lat_lo[:]

        def act_split_first_hidden(a, name):
            if name == "down1":
                a.wait_ge(*freed("gu1", 2))
            else:
                a.wait_ge(hidden_ready, 2 + FC * (name == "down3") + 1)
            a.activation(first_hi, big[:, 0, :], ACT.Copy).then_inc(hi_ready, 1)

        def dve_split_first_hidden(v, name):
            v.wait_ge(hi_ready, SPLIT_AT[name] + 1)
            v.tensor_tensor(first_lo, big[:, 0, :], f32(first_hi), ALU.subtract).then_inc(lo_ready, 1)

        def act_split_hidden(a, name):
            for t in range(1, FC):
                if t == 1:
                    a.wait_ge(block_done, START[name])
                if t >= 5:
                    a.wait_ge(block_done, START[name] + t - 3)
                if name == "down1":
                    a.wait_ge(*freed("gu1", 2 * t + 2))
                else:
                    a.wait_ge(hidden_ready, 2 + FC * (name == "down3") + t + 1)
                a.activation(a_hi[:, t % 4, :], big[:, t, :], ACT.Copy).then_inc(hi_ready, 1)

        def dve_split_hidden(v, name):
            for t in range(1, FC):
                v.wait_ge(hi_ready, SPLIT_AT[name] + t + 1)
                v.tensor_tensor(a_lo[:, t % 4, :], big[:, t, :], f32(a_hi[:, t % 4, :]), ALU.subtract).then_inc(lo_ready, 1)

        def wait_down(e, n, c):
            if c < DC - 1:
                e.wait_ge(down_done, (DC - 1) * n + c + 1)
            else:
                e.wait_ge(block_done, START[("down1", "down2", "down3")[n]] + FC)

        block = ctx.enter_context(nc.Block())

        @block.sync
        def _(sp):
            for j in range(X_PARTS):
                part = slice(j * DC // X_PARTS, (j + 1) * DC // X_PARTS)
                sp.dma_start(x[:, part, :], x_in[:, part, :]).then_inc(x_landed[j], 16)
            sp.dma_start(vecs[:], vecs_in).then_inc(vecs_landed, 16)
            for j in range(RAW):
                sp.dma_start(raw[:, j, :], stream_in[j]).then_inc(raw_landed[j], 16)

            def load(j, b):
                sp.wait_ge(split_ready, b - (RAW - 1))
                sp.dma_start(raw[:, j, :], stream_in[bass.ds(b, 1)].rearrange("o p n -> (o p) n")).then_inc(raw_landed[j], 16)
            with sp.Fori(1, N_BLOCKS // RAW) as r:
                for j in range(RAW):
                    load(j, r * RAW + j)
            for b in range(N_BLOCKS // RAW * RAW, N_BLOCKS):
                load(b % RAW, b)
            for c in range(DC):
                sp.wait_ge(x_ready, X_AT["down3"] + c + 1)
                sp.dma_start(out[:, c, :], x[:, c, :]).then_inc(out_stored, 16)
            sp.wait_ge(out_stored, 16 * DC)

        @block.gpsimd
        def _(pool):
            def split(j, s, b, turn, wait=True):
                pool.wait_ge(raw_landed[j], turn * 16 + 16)
                if wait:
                    pool.wait_ge(block_done, b - (SPLIT - 1))
                pool.sem_inc(split_begun, 1)
                pool.tensor_scalar(w_hi[:, s, :], raw[:, j, :], 1.0, 1.0, ALU.mult, ALU.mult).then_inc(high_ready, 1)
                pool.wait_ge(high_ready, b + 1)
                pool.tensor_tensor(w_lo[:, s, :], raw[:, j, :], f32(w_hi[:, s, :]), ALU.subtract).then_inc(split_ready, 1)

            def pool_lows(name):
                for c in range(1, DC, 2):
                    write_low(pool, lo_pool_ready, name, c)

            def split_stream(first, end):
                turns = (end - first) // RAW
                with pool.Fori(0, turns) as r:
                    for j in range(first, first + RAW):
                        split(j % RAW, j % SPLIT, r * RAW + j, r + j // RAW)
                for b in range(first + turns * RAW, end):
                    split(b % RAW, b % SPLIT, b, b // RAW)

            pool.memset(big[64:P, 0:A_HEADS:2, :], 0.0).then_inc(zeroed, 1)
            pool.wait_ge(zeroed, 1)
            pool.memset(big[0:64, 1:A_HEADS:2, :], 0.0).then_inc(zeroed, 1)
            pool.wait_ge(zeroed, 2)
            for b in range(SPLIT):
                split(b, b, b, 0, wait=False)
            pool_lows("pre_mix")
            split_stream(SPLIT, START["gu1"] + SPLIT)
            pool_lows("pre_ffn")
            split_stream(START["gu1"] + SPLIT, START["bq"] + SPLIT)
            pool.wait_ge(x_ready, X_AT["pe_gate"] + DC)
            pool.wait_ge(split_ready, START["bq"] + SPLIT)
            pool.memset(big[64:P, 0:B_HEADS:2, :], 0.0).then_inc(zeroed, 1)
            pool.wait_ge(zeroed, 3)
            pool.memset(big[0:64, 1:B_HEADS:2, :], 0.0).then_inc(zeroed, 1)
            pool.wait_ge(zeroed, 4)
            pool_lows("mix0")
            split_stream(START["bq"] + SPLIT, START["out2"] + SPLIT)
            for h in range(B_HEADS):
                for n in (1, 2, 0):
                    pool.wait_ge(b_hi, 3 * h + (1, 2, 0).index(n) + 1)
                    if h >= 2 and n == 1:
                        pool.wait_ge(b_e, 3 * (h - 1))
                    pool.tensor_tensor(sp_low(h, n), soft_buf(h, n), f32(sp_high(h, n)), ALU.subtract).then_inc(b_lo, 1)
            split_stream(START["out2"] + SPLIT, START["gu2"] + SPLIT)
            pool_lows("ffn0")
            split_stream(START["gu2"] + SPLIT, START["qi"] + SPLIT)
            pool_lows("mix1")
            split_stream(START["qi"] + SPLIT, START["gu3"] + SPLIT)
            pool_lows("ffn1")
            split_stream(START["gu3"] + SPLIT, N_BLOCKS)

        @block.tensor
        def _(pe):
            pe.wait_ge(masks_ready, 4)
            pe_norm(pe, "pre_mix")
            pe.wait_ge(onehot_landed, 32)
            big_flat = big[:].rearrange("p c s -> p (c s)")
            for n in range(2):
                m = pe.matmul(bank[6 + n][0:D_HEADS, 0:SPAN // 2], big_flat[0:BUCKETS, 20 * S + SPAN:20 * S + SPAN + D_HEADS],
                              big_flat[0:BUCKETS, 20 * S + n * (SPAN // 2):20 * S + (n + 1) * (SPAN // 2)], start=True, stop=True)
            m.then_inc(rel_row, 1)
            pe_token_tiles(pe, "z")
            pe_tiles(pe, "u")
            pe_tiles(pe, "q")
            pe.wait_ge(z_normed, 2 * 16 + TT)
            pe.wait_ge(ws_masked, 1)
            for g in range(GROUPS):
                if g == 3:
                    pe.wait_ge(mixed_step, 1)
                for i in range(TT):
                    m = pe.matmul(bank[5 + g % 3][:, i * P:(i + 1) * P], big[:, 16 + i, g * P:(g + 1) * P], ws[:, g, :],
                                  start=True, stop=True)
                m.then_inc(mixed_ready, 1)
            pe_tiles(pe, "k")
            pe_token_tiles(pe, "v")
            pe_sum_group(pe, "sgu", 0)
            pe.wait_ge(*freed("v", 4))
            pe.wait_ge(mixed_step, 4)
            pe.wait_ge(zeroed, 2)
            pe_attention(pe, a_sems, a_units,
                         lambda h, i: big[:, h, i * P:(i + 1) * P],
                         lambda h, cols: big[:, 16 + h // 2, 0:cols],
                         lambda h, j: big[:, 8 + j, h * A_HD:(h + 1) * A_HD],
                         lambda u: y[:, u % 4, :], None, lambda c: (a_sems["evac"], c + 1))
            pe_spread(pe, "sgu")
            for g in range(2):
                pe_sum_group(pe, "attn", g)
            pe_tiles(pe, "out1", "attn", norm="post_mix")
            pe_norm(pe, "post_mix", 1)
            pe_norm(pe, "pre_ffn")
            pe_tiles(pe, "gu1", "pre_ffn")
            pe_down(pe, "down1", 0, norm="post_ffn")
            for g in range(2, 5):
                pe_sum_group(pe, "post_ffn", g)
            pe.wait_ge(down_taken, 8)
            pe.wait_ge(inverse_step, 5 * NORM_INDEX["post_ffn"] + 1)
            pe_begin(pe, "pe_proj")
            pe.wait_ge(*low_done("p", 1))
            for b in range(2):
                s = (START["pe_proj"] + b) % SPLIT
                pe.wait_ge(split_ready, START["pe_proj"] + b + 1)
                for t in range(4):
                    pe.wait_ge(*freed("pe_proj", 4 * b + t - 3))
                    for k in range(2):
                        o = (2 * t + k) * P
                        m = pe_three_passes(pe, bank[t][:], w_hi[:, s, o:o + P], w_lo[:, s, o:o + P],
                                            a_hi[:, 4 + k, :], a_lo[:, 4 + k, :], k == 0, k == 1)
                    m.then_inc(*((pe_ready, 1) if t < 3 else (block_done, 1)))
                    if b == 0 and t == 1:
                        pe_spread(pe, "post_ffn")
            pe_tiles(pe, "pe_gate", "pe_gate")
            pe_norm(pe, "mix0")
            pe_tiles(pe, "bq", "mix0")
            pe_tiles(pe, "bk")
            pe_token_tiles(pe, "bv", 2)
            pe.wait_ge(*freed("bv", 8))
            pe.wait_ge(zeroed, 4)
            pe_stick(pe)
            pe_tiles(pe, "out2", "battn", norm="ffn0")
            pe_norm(pe, "ffn0", 1)
            pe_tiles(pe, "gu2", "ffn0")
            pe_down(pe, "down2", 1, norm="mix1")
            pe_norm(pe, "mix1", 2)
            pe_tiles(pe, "qi", "mix1")
            pe_tiles(pe, "ki")
            pe.wait_ge(wi_split, 2)
            for t in range(TT):
                for k in range(DC):
                    m = pe_three_passes(pe, bank[7][:, t * 8:(t + 1) * 8], a_hi[:, k, t * P:(t + 1) * P],
                                        a_lo[:, k, t * P:(t + 1) * P], wi_hi[:, k, :], wi_lo[:, k, :], k == 0, k == DC - 1)
            m.then_inc(wi_ready, 1)

            def index_scores(n):
                i, h = 1 + n // IDX_HEADS, n % IDX_HEADS
                cols = P * (i + 1)
                if n == 0:
                    pe.wait_ge(*freed("ki", 1))
                    pe.wait_ge(index_init, 8)
                if n >= 2:
                    pe.wait_ge(relu_ready, n - 1)
                pe.matmul(bank[(4, 6)[n % 2]][:, 0:cols], big[:, 16 + h // 2, i * P:(i + 1) * P], tmp[:, 2 + h % 2, 0:cols],
                          start=True, stop=True).then_inc(index_ready, 1)

            def head_sum(m):
                pe.wait_ge(qsq_ready, m + 1)
                for t in range(TT):
                    p = pe.matmul(head_sums[:, m * TT + t:m * TT + t + 1], tmp[:, m % 2, t * P:(t + 1) * P], ones[:, 0:1],
                                  start=t == 0, stop=True, skip_group_check=True)
                p.then_inc(qsum_ready, 1)
            pe_begin(pe, "lat")
            pe_tile(pe, "lat", 0, 0)
            for i in range(D_HEADS):
                pe_tile(pe, "dq", i % 4, i, first_bank=1)
                if i == 1:
                    pe.wait_ge(k_diag_ready, 1)
                    pe.matmul(rstd_bank[:], ones, diag[:].rearrange("p t i -> p (t i)"), start=True, stop=True).then_inc(k_rstd_ready, 1)
                head_sum(i)
                for n in range(4 * i, min(4 * i + 4, 3 * IDX_HEADS)):
                    index_scores(n)
            head_sum(D_HEADS)
            pe_begin(pe, "uv")
            pe.wait_ge(lat_split, 3)
            s = START["uv"] % SPLIT
            pe.wait_ge(split_ready, START["uv"] + 1)
            for h in range(2):
                for t in range(TT):
                    pe.wait_ge(*freed("uv", 4 * h + t - 3))
                    m = pe_three_passes(pe, bank[t][:], lat_hi[:, t * P:(t + 1) * P], lat_lo[:, t * P:(t + 1) * P],
                                        w_hi[:, s, h * S:(h + 1) * S], w_lo[:, s, h * S:(h + 1) * S], True, True)
                    if h == 0 or t < 3:
                        m.then_inc(uv_ready, 1)
            m.then_inc(block_done, 1)
            pe.wait_ge(*freed("uv", 8))
            pe.wait_ge(selected, 4)
            pe.wait_ge(k_scaled, 1)
            pe.wait_ge(inverse_step, 5 * 10 + 1)
            pe_attention(pe, d_sems, d_units,
                         lambda h, i: big[:, h, i * P:(i + 1) * P],
                         lambda h, cols: k_lat[:, 0:cols],
                         lambda h, j: big[:, 16 + 2 * j + h // 8, 64 * (h % 8):64 * (h % 8) + 64],
                         lambda u: probs_t[:, u % 4, :],
                         lambda i, cols: not_selected[:, i, 0:cols],
                         lambda c: low_done("dattn", c), read="scaled")
            pe_tiles(pe, "out3", "dattn", norm="ffn1")
            pe_norm(pe, "ffn1", 1)
            pe_tiles(pe, "gu3", "ffn1")
            pe_down(pe, "down3", 2)

        def act_tile(a, name, n, b, dst, func=ACT.Copy, **kw):
            a.wait_ge(block_done, b + 1)
            a.activation(dst, bank[n % 4][:], func, **kw).then_inc(banks_free["act"], 1)

        def act_query_pair(a, name, c, scale):
            a.wait_ge(block_done, START[name] + c + 1)
            for half in range(2):
                rows = slice(64 * half, 64 * half + 64)
                m = a.activation(big[rows, 2 * c + half, :], bank[c % 4][rows, :], ACT.Copy, scale=scale)
            m.then_inc(banks_free["act"], 1)

        def ada_load(a, n, m):
            a.dma_start(y_flat[:, m * D:(m + 1) * D], ada_in[bass.ds(n, 1)].rearrange("o p k -> (o p) k")).then_inc(ada_landed[m], 16)

        def act_conv(a, layer):
            phase = "gu2" if layer == 0 else "gu3"
            a.preload_act_table(ACT.Silu)
            def turn(r, split=False):
                for jj in range(2):
                    a.wait_ge(hidden_ready, layer * FC + jj + 1 + 2 * r)
                    for g in range(2):
                        n = 2 * jj + g
                        col = VEC["conv"] + (layer * FC + jj) * 8 + 4 * g
                        a.wait_ge(block_done, START[phase] + n + 1 + 4 * r)
                        a.activation(tmp[:, n, :], bank[n][:], ACT.Identity, bias=vecs[:, bass.ds(r * 16 + (col + 3), 1)],
                                     scale=vecs[:, bass.ds(r * 16 + (col + 2), 1)]).then_inc(conv_base, 1)
                    counter, value = freed(phase, 2 * jj + 1)
                    a.wait_ge(counter, value + 4 * r)
                    a.activation(tmp[:, 2 * jj, :], tmp[:, 2 * jj, :], ACT.Silu).then_inc(silu_ready, 1)
                    if split and jj == 0:
                        act_split_first_hidden(a, "down2" if layer == 0 else "down3")
            with a.Fori(0, FC // 2 - 1) as r:
                turn(r)
            turn(FC // 2 - 1, split=True)

        def act_x_square(a, name, update, c):
            a.wait_ge(x_ready, X_AT[update] + c + 1)
            act_square(a, name, c, x[:, c, :])

        def act_x_squares(a, name, update):
            act_squares(a, name, [x[:, c, :] for c in range(DC)], lambda c: (x_ready, X_AT[update] + c + 1))

        def act_stream_squares(a, name, n, tile_ready, done):
            for c in range(DC):
                tile_ready(c)
                b = bank[c % n][:]
                act_square(a, name, c, b)
                a.activation(y[:, c, :], b, ACT.Copy).then_inc(done, 1)

        @block.scalar
        def _(a):
            a.dma_start(consts[:], consts_in).then_inc(consts_landed, 16)
            a.sem_inc(banks_free["act"], 4)
            a.sem_inc(banks_free["dve"], 4)
            a.sem_inc(hidden_ready, 2)
            act_squares(a, "pre_mix", [x[:, c, :] for c in range(DC)], lambda c: (x_landed[c * X_PARTS // DC], 16))
            a.preload_act_table(ACT.Sqrt)
            a.dma_start(big[0:BUCKETS, 20:22, :].rearrange("p c s -> p (c s)")[:, 0:SPAN], onehot_in).then_inc(onehot_landed, 16)
            a.dma_start(big[0:BUCKETS, 20:22, :].rearrange("p c s -> p (c s)")[:, SPAN:SPAN + D_HEADS], rel_in).then_inc(onehot_landed, 16)
            act_rms(a, "pre_mix")
            a.dma_start(sgu_g[:], sgu_g_in.partition_broadcast(P)).then_inc(rows_landed, 16)
            a.dma_start(sgu_b[:], sgu_b_in.partition_broadcast(P)).then_inc(rows_landed, 16)
            a.dma_start(bs[:].rearrange("p g i -> p (g i)"), bs_in.partition_broadcast(P)).then_inc(rows_landed, 16)
            a.dma_start(ws[:], ws_in).then_inc(rows_landed, 16)
            a.dma_start(cond[:], c_in.partition_broadcast(P)).then_inc(cond_landed, 16)
            a.dma_start(wi_raw[:], wi_in).then_inc(wi_landed, 16)
            a.dma_start(bias[:], bias_in).then_inc(bias_landed, 16)
            a.dma_start(big[:, 22:24, :], p_in).then_inc(p_landed, 16)
            act_high(a, "pre_mix", DC)
            a.wait_ge(rel_row, 1)
            for n in range(2):
                a.activation(y_flat[0:D_HEADS, n * (SPAN // 2):(n + 1) * (SPAN // 2)], bank[6 + n][0:D_HEADS, 0:SPAN // 2],
                             ACT.Copy).then_inc(rel_copied, 1)
            a.wait_ge(rel_copied, 2)
            a.dma_start(scratch, y_flat[0:D_HEADS, 0:SPAN]).then_inc(rel_stored, 16)
            for t in range(TT):
                act_tile(a, "z", t, START["z"] + 3, big[:, 16 + t, :], ACT.Gelu_apprx_tanh)
            for c in range(4):
                act_tile(a, "u", c, START["u"] + c, big[:, 12 + c, :], ACT.Gelu_apprx_tanh)
            a.wait_ge(cond_landed, 16)
            a.activation(cond[:], cond[:], ACT.Silu).then_inc(cond_ready, 1)
            a.wait_ge(rel_stored, 16)
            for n in range(4):
                ada_load(a, n, n)
            a.wait_ge(z_step, 33)
            a.activation(z_rstd[:], z_rstd[:], ACT.Sqrt).then_inc(z_std, 1)
            for c in range(4):
                act_query_pair(a, "q", c, A_HD ** -0.5)
            for n in range(4, ADA_STEP):
                a.wait_ge(ada_done, n - 3)
                ada_load(a, n, n - 4)
            a.wait_ge(mixed_ready, GROUPS)
            for c in range(4):
                act_tile(a, "k", c, START["k"] + c, big[:, 16 + c, :])
            act_squares(a, "sgu", [big[:, 12 + c, :] for c in range(4)], lambda c: (sgu_ready, c + 1))
            for t in range(TT):
                act_tile(a, "v", t, START["v"] + 3, big[:, 8 + t, :])
            act_rms(a, "sgu")

            def a_evacuate(a, c):
                a.activation(big[:, c, :], bank[6 + c % 2][:], ACT.Copy).then_inc(a_sems["evac"], 1)
            act_attention(a, a_sems, a_units, lambda u: y[:, u % 4, :], 0, a_evacuate)
            act_squares(a, "attn", [big[:, c, :] for c in range(4)], lambda c: (a_sems["evac"], c + 1))
            act_high(a, "sgu", 4, first=4)
            act_rms(a, "attn")
            act_high(a, "attn", 4)
            act_stream_squares(a, "post_mix", 4, lambda c: a.wait_ge(block_done, START["out1"] + c + 1), banks_free["act"])
            act_rms(a, "post_mix")
            act_x_squares(a, "pre_ffn", "post_mix")
            act_rms(a, "pre_ffn")
            act_high(a, "pre_ffn", DC)
            a.preload_act_table(ACT.Silu)

            def silu_turn(r, split=False):
                for jj in range(2):
                    for m in range(4):
                        a.wait_ge(ada_done, r * ADA_STEP + (ADA_STEP + 4 * jj + m - 3))
                        ada_load(a, r * ADA_STEP + (ADA_STEP + 4 * jj + m), m)
                    a.wait_ge(block_done, START["gu1"] + 2 * jj + 1 + 4 * r)
                    a.activation(tmp[:, 2 * jj, :], bank[2 * jj][:], ACT.Silu).then_inc(silu_ready, 1)
                    if split and jj == 0:
                        act_split_first_hidden(a, "down1")
            with a.Fori(0, FC // 2 - 1) as r:
                silu_turn(r)
            silu_turn(FC // 2 - 1, split=True)
            act_split_hidden(a, "down1")
            a.wait_ge(p_landed, 16)
            for k in range(2):
                a.activation(a_hi[:, 4 + k, :], big[:, 22 + k, :], ACT.Copy).then_inc(hi_ready, 1)
            a.wait_ge(ada_done, 2 * MOD)
            act_stream_squares(a, "post_ffn", 8, lambda c: wait_down(a, 0, c), down_taken)
            act_rms(a, "post_ffn")
            for c in range(DC):
                if c % 4 < 3:
                    a.wait_ge(pe_ready, 3 * (c // 4) + c % 4 + 1)
                else:
                    a.wait_ge(block_done, START["pe_proj"] + c // 4 + 1)
                a.activation(big[:, c, :], bank[c % 4][:], ACT.Copy).then_inc(banks_free["act"], 1)
            for c in range(DC):
                a.wait_ge(x_ready, X_AT["post_ffn"] + c + 1)
                a.activation(a_hi[:, c, :], x[:, c, :], ACT.Copy).then_inc(hi_ready, 1)
            for c in range(DC):
                if c >= 4:
                    a.wait_ge(x_ready, X_AT["pe_gate"] + c - 3)
                act_tile(a, "pe_gate", c, START["pe_gate"] + c, tmp[:, c % 4, :], ACT.Sigmoid, bias=vec("b_pe_gate", c))
                if c:
                    act_x_square(a, "mix0", "pe_gate", c - 1)
            act_x_square(a, "mix0", "pe_gate", DC - 1)
            act_rms(a, "mix0")
            a.wait_ge(mods_ready, 1)
            act_high(a, "mix0", DC, shift=lambda c: mod(0, 0, c))
            for c in range(8):
                act_query_pair(a, "bq", c, B_HD ** -0.5)
            for c in range(8):
                act_tile(a, "bk", c, START["bk"] + c, big[:, 16 + c, :])
            for h in range(2):
                for t in range(TT):
                    act_tile(a, "bv", t, START["bv"] + 4 * h + 3, (tmp, probs_t)[h][:, t, :])
            act_stick(a)
            a.wait_ge(b_e, 3 * B_HEADS)
            for c in range(DC):
                a.wait_ge(b_evac, 2 * c + 2)
                a.activation(a_hi[:, c, :], big[:, 2 * c, :], ACT.Copy).then_inc(hi_ready, 1)
            a.wait_ge(b_out, B_HEADS)
            for n, dst in enumerate((y, bias)):
                src = bass.AP(tensor=scratch.tensor, offset=8 * n * SPAN, ap=[[1, P], [SPAN, 8], [1, S]])
                a.dma_start(dst[:], src).then_inc(tables_landed, 16)
            act_x_squares(a, "ffn0", "out2")
            act_rms(a, "ffn0")
            act_high(a, "ffn0", DC, shift=lambda c: mod(0, 3, c))
            act_conv(a, 0)
            act_split_hidden(a, "down2")
            act_x_squares(a, "mix1", "down2")
            act_rms(a, "mix1")
            act_high(a, "mix1", DC, shift=lambda c: mod(1, 0, c))
            for c in range(4):
                act_tile(a, "qi", c, START["qi"] + c, big[:, 16 + c, :])
            a.wait_ge(block_done, START["ki"] + 1)
            a.activation(tmp[0:64, 2, :], bank[0][0:64, :], ACT.Copy)
            a.activation(tmp[64:P, 3, :], bank[0][64:P, :], ACT.Copy).then_inc(banks_free["act"], 1)
            a.wait_ge(wi_ready, 1)
            a.activation(wi[:].rearrange("p t h -> p (t h)"), bank[7][:, 0:TT * IDX_HEADS], ACT.Copy,
                         scale=IDX_HEADS ** -0.5).then_inc(wi_taken, 1)

            def head_square(m):
                b = START["lat"] if m == 0 else START["dq"] + m - 1
                a.wait_ge(block_done, b + 1)
                if m >= 2:
                    a.wait_ge(qsum_ready, m - 1)
                a.activation(tmp[:, m % 2, :], bank[m % 4][:], ACT.Square).then_inc(qsq_ready, 1)
                if m == 0:
                    a.activation(lat_hi[:], bank[0][:], ACT.Copy).then_inc(lat_split, 1)
                a.activation(k_lat[:] if m == 0 else big[:, m - 1, :], bank[m % 4][:], ACT.Copy).then_inc(banks_free["act"], 1)

            def index_relu(n):
                cols = P * (2 + n // IDX_HEADS)
                a.wait_ge(index_ready, n + 1)
                if n >= 4:
                    a.wait_ge(index_added, n - 3)
                a.activation(probs_t[:, n % 4, 0:cols], bank[(4, 6)[n % 2]][:, 0:cols], ACT.Relu).then_inc(relu_ready, 1)
            head_square(0)
            for m in range(1, D_HEADS + 1):
                head_square(m)
                if m == 1:
                    a.wait_ge(inverse_step, 5 * 9 + 1)
                    a.activation(rms[:, 0, :], rms[:, 1, :], ACT.Sqrt).then_inc(qrms_ready, 1)
                for n in range(4 * m - 4, min(4 * m, 3 * IDX_HEADS)):
                    index_relu(n)
            a.wait_ge(inverse_step, 5 * 10 + 1)
            a.activation(q_rms[:, 0, :], q_rms[:, 1, :], ACT.Sqrt).then_inc(qrms_ready, 1)
            a.wait_ge(selected, 4)
            for h in range(2):
                for t in range(TT):
                    if h == 0 or t < 3:
                        a.wait_ge(uv_ready, 4 * h + t + 1)
                    else:
                        a.wait_ge(block_done, START["uv"] + 1)
                    a.activation(big[:, 16 + 2 * t + h, :], bank[t][:], ACT.Copy).then_inc(banks_free["act"], 1)

            def d_evacuate(a, c):
                a.activation(a_hi[:, c, :], bank[6 + c % 2][:], ACT.Copy).then_inc(hi_ready, 1)
            a.wait_ge(inverse_step, 5 * 11)
            act_attention(a, d_sems, d_units, lambda u: probs_t[:, u % 4, :], n_stat // 2, d_evacuate,
                          scale=lambda h, i: q_rms[:, 1, h * TT + i:h * TT + i + 1])
            act_x_squares(a, "ffn1", "out3")
            act_rms(a, "ffn1")
            act_high(a, "ffn1", DC, shift=lambda c: mod(1, 3, c))
            act_conv(a, 1)
            act_split_hidden(a, "down3")

        def dve_post_norm(v, name, n, norm=None):
            g = "ln_" + name
            for c in range(DC + 1):
                if c < DC:
                    v.scalar_tensor_tensor(tmp[:, c % 4, :], y[:, c, :], vec(g, c), rstd_bank[:], ALU.mult, ALU.mult).then_inc(post_step, 1)
                if c >= 1:
                    v.wait_ge(post_step, DC * n + c)
                    v.tensor_tensor(x[:, c - 1, :], x[:, c - 1, :], tmp[:, (c - 1) % 4, :], ALU.add).then_inc(x_ready, 1)
                if norm and c >= 2:
                    dve_add_square(v, norm, c - 2)
            if norm:
                dve_add_square(v, norm, DC - 1)

        def dve_ada(v, n, m, part):
            w = y_flat[:, m * D:(m + 1) * D]
            v.tensor_tensor_reduce(w, w, cond[:], 1.0, 0.0, ALU.mult, ALU.add, ada_part[:, part:part + 1]).then_inc(ada_done, 1)

        def dve_conv(v, layer):
            phase = "gu2" if layer == 0 else "gu3"
            def turn(r, split=False):
                for jj in range(2):
                    for g in range(2):
                        n = 2 * jj + g
                        col = VEC["conv"] + (layer * FC + jj) * 8 + 4 * g
                        v.wait_ge(conv_base, layer * 2 * FC + n + 1 + 4 * r)
                        v.scalar_tensor_tensor(tmp[:, n, 1:S], bank[n][:, 0:S - 1], vecs[:, bass.ds(r * 16 + (col + 1), 1)],
                                               tmp[:, n, 1:S], ALU.mult, ALU.add).then_inc(conv_step, 1)
                        v.wait_ge(conv_step, layer * 2 * FC + n + 1 + 4 * r)
                        v.scalar_tensor_tensor(tmp[:, n, 2:S], bank[n][:, 0:S - 2], vecs[:, bass.ds(r * 16 + col, 1)],
                                               tmp[:, n, 2:S], ALU.mult, ALU.add).then_inc(banks_free["dve"], 1)
                    counter, value = freed(phase, 2 * jj + 2)
                    v.wait_ge(counter, value + 4 * r)
                    v.wait_ge(silu_ready, FC + layer * FC + jj + 1 + 2 * r)
                    v.tensor_tensor(big[:, bass.ds(r * 2 + jj, 1), :].rearrange("p o s -> p (o s)"), tmp[:, 2 * jj, :],
                                    tmp[:, 2 * jj + 1, :], ALU.mult).then_inc(hidden_ready, 1)
                    if split and jj == 0:
                        dve_split_first_hidden(v, "down2" if layer == 0 else "down3")
            with v.Fori(0, FC // 2 - 1) as r:
                turn(r)
            turn(FC // 2 - 1, split=True)

        def dve_residual(v, update, layer, which, ready, n, norm=None):
            slow = n == 4
            for c in range(DC):
                if norm and c and slow:
                    dve_add_square(v, norm, c - 1)
                ready(c)
                v.scalar_tensor_tensor(x[:, c, :], bank[c % n][:], mod(layer, which, c), x[:, c, :], ALU.mult,
                                       ALU.add).then_inc(x_ready, 1)
                if norm and c and not slow:
                    dve_add_square(v, norm, c - 1)
            if norm:
                dve_add_square(v, norm, DC - 1)

        @block.vector
        def _(v):
            v.wait_ge(consts_landed, 16)
            v.tensor_copy(ident_b[:], ident).then_inc(masks_ready, 1)
            v.tensor_copy(strict_b[:], strict).then_inc(masks_ready, 1)
            v.tensor_copy(neg_ones_r[:], neg_ones).then_inc(masks_ready, 1)
            v.tensor_copy(neg_suffix_r[:], neg_suffix).then_inc(masks_ready, 1)
            dve_diag(v, "pre_mix")
            v.wait_ge(vecs_landed, 16)
            dve_scale_split(v, "pre_mix", "pre_mix", DC, lambda c: x[:, c, :], lambda c: vec("ln_pre_mix", c))
            v.wait_ge(rows_landed, 64)
            v.tensor_tensor(ws[:], ws[:], upper.unsqueeze(1).broadcast_to([P, GROUPS, P]), ALU.mult).then_inc(ws_masked, 1)
            for t in range(TT):
                v.wait_ge(*freed("z", t + 1))
                for g in range(GROUPS):
                    v.bn_stats(z_stat[:, 4 * t + g, :], big[:, 16 + t, g * P:(g + 1) * P]).then_inc(z_step, 1)
            for n in range(16):
                v.wait_ge(z_step, 16)
                v.bn_aggr(z_mv[:, n, :], z_stat[:, n, :]).then_inc(z_normed, 1)
            v.wait_ge(z_normed, 16)
            v.tensor_scalar(z_rstd[:], z_mv[:, :, 1], EPS, None, ALU.add).then_inc(z_step, 16)
            v.wait_ge(z_step, 32)
            v.reciprocal(z_rstd[:], z_rstd[:]).then_inc(z_step, 1)
            v.wait_ge(z_std, 1)
            for n in range(16):
                t, g = n // 4, n % 4
                zg = big[:, 16 + t, g * P:(g + 1) * P]
                v.tensor_scalar(zg, zg, z_mv[:, n, 0:1], z_rstd[:, n:n + 1], ALU.subtract, ALU.mult).then_inc(z_normed, 1)
            for t in range(TT):
                zt = big[:, 16 + t, :].rearrange("p (g i) -> p g i", g=GROUPS)
                v.wait_ge(z_normed, 16 + 4 * t + 4)
                v.tensor_tensor(zt, zt, sgu_g[:].unsqueeze(1).broadcast_to([P, GROUPS, P]), ALU.mult).then_inc(z_step, 1)
            for t in range(TT):
                zt = big[:, 16 + t, :].rearrange("p (g i) -> p g i", g=GROUPS)
                v.wait_ge(z_step, 33 + t + 1)
                v.tensor_tensor(zt, zt, sgu_b[:].unsqueeze(1).broadcast_to([P, GROUPS, P]), ALU.add).then_inc(z_normed, 1)
            for g in range(GROUPS):
                v.wait_ge(mixed_ready, g + 1)
                v.tensor_tensor(tmp[:, g, :].rearrange("p (t i) -> p t i", t=TT), bank[5 + g % 3][:].rearrange("p (t i) -> p t i", t=TT),
                                bs[:, g, :].unsqueeze(1).broadcast_to([P, TT, P]), ALU.add).then_inc(mixed_step, 1)
                v.wait_ge(mixed_step, g + 1)
                if g == 0:
                    v.wait_ge(*freed("u", 4))
                v.tensor_tensor(big[:, 12 + g, :], big[:, 12 + g, :], tmp[:, g, :], ALU.mult).then_inc(sgu_ready, 1)
            v.wait_ge(cond_ready, 1)
            for n in range(ADA_STEP):
                v.wait_ge(ada_landed[n % 4], 16 * (n // 4 + 1))
                dve_ada(v, n, n % 4, n)
            v.wait_ge(ada_done, ADA_STEP)
            v.tensor_copy(mods[:, 0:ADA_STEP], ada_part[:]).then_inc(ada_copied, 1)
            dve_diag(v, "sgu", wait=False)
            v.wait_ge(bias_landed, 16)
            dve_attention(v, a_sems, a_units, lambda h, cols: bias[:, h, S - cols:S], 0)
            dve_add_squares(v, "attn")
            v.wait_ge(rstd_ready, NORM_INDEX["sgu"] + 1)
            dve_scale_split(v, "sgu", "sgu", 4, lambda c: big[:, 12 + c, :], lambda c: vec("sgu_out_norm", c), first=4)
            dve_diag(v, "attn", add=False)
            dve_scale_split(v, "attn", "attn", 4, lambda c: big[:, c, :], lambda c: vec("attn_out_norm", c))
            dve_diag(v, "post_mix")
            dve_post_norm(v, "post_mix", 0, "pre_ffn")
            dve_diag(v, "pre_ffn", add=False)
            dve_scale_split(v, "pre_ffn", "pre_ffn", DC, lambda c: x[:, c, :], lambda c: vec("ln_pre_ffn", c))
            def product_turn(r, split=False):
                for jj in range(2):
                    v.wait_ge(silu_ready, jj + 1 + 2 * r)
                    v.wait_ge(block_done, START["gu1"] + 2 * jj + 2 + 4 * r)
                    v.tensor_tensor(big[:, bass.ds(r * 2 + jj, 1), :].rearrange("p o s -> p (o s)"), tmp[:, 2 * jj, :],
                                    bank[2 * jj + 1][:], ALU.mult).then_inc(banks_free["dve"], 2)
                    if split and jj == 0:
                        dve_split_first_hidden(v, "down1")
                    for m in range(4):
                        v.wait_ge(ada_landed[m], r * 32 + 16 * (3 + jj))
                        if jj == 0 and m == 0:
                            v.wait_ge(ada_copied, r + 1)
                        dve_ada(v, None, m, 4 * jj + m)
                v.wait_ge(ada_done, r * ADA_STEP + 2 * ADA_STEP)
                v.tensor_copy(mods[:, bass.ds(r * ADA_STEP + ADA_STEP, ADA_STEP)], ada_part[:]).then_inc(ada_copied, 1)
            with v.Fori(0, FC // 2 - 1) as r:
                product_turn(r)
            product_turn(FC // 2 - 1, split=True)
            v.wait_ge(ada_copied, 2 * MOD // ADA_STEP)
            v.tensor_tensor(mods[:], mods[:], vec("ada_b_2", 0, 2 * MOD), ALU.add).then_inc(mods_ready, 1)
            v.wait_ge(mods_ready, 1)
            for n in range(4):
                layer, which = n // 2, (1, 4)[n % 2]
                name = ("norm_mix_2", "norm_ffn_2")[n % 2]
                at = layer * MOD + which * DC
                v.scalar_tensor_tensor(gains[:, n, :], mods[:, at:at + DC], 1.0, vec(name, layer * DC, DC), ALU.add,
                                       ALU.mult).then_inc(mods_ready, 1)
            dve_split_hidden(v, "down1")
            for k in range(2):
                v.wait_ge(hi_ready, SPLIT_AT["p"] + k + 1)
                v.tensor_tensor(a_lo[:, 4 + k, :], big[:, 22 + k, :], f32(a_hi[:, 4 + k, :]), ALU.subtract).then_inc(lo_ready, 1)
            dve_diag(v, "post_ffn")
            dve_post_norm(v, "post_ffn", 1)
            for c in range(DC):
                v.wait_ge(hi_ready, SPLIT_AT["pe_gate"] + c + 1)
                v.tensor_tensor(a_lo[:, c, :], x[:, c, :], f32(a_hi[:, c, :]), ALU.subtract).then_inc(lo_ready, 1)
            for c in range(DC):
                v.wait_ge(*freed("pe_gate", c + 1))
                v.tensor_tensor(tmp[:, c % 4, :], tmp[:, c % 4, :], big[:, c, :], ALU.mult).then_inc(gate_step, 1)
                v.wait_ge(gate_step, c + 1)
                v.tensor_tensor(x[:, c, :], x[:, c, :], tmp[:, c % 4, :], ALU.add).then_inc(x_ready, 1)
                if c:
                    dve_add_square(v, "mix0", c - 1)
            dve_add_square(v, "mix0", DC - 1)
            dve_diag(v, "mix0", add=False)
            v.wait_ge(mods_ready, 5)
            dve_scale_split(v, "mix0", "mix0", DC, lambda c: x[:, c, :], lambda c: gains[:, 0, c:c + 1], lambda c: mod(0, 0, c))
            dve_stick(v)
            for c in range(DC):
                v.wait_ge(hi_ready, SPLIT_AT["battn"] + c + 1)
                v.tensor_tensor(a_lo[:, c, :], big[:, 2 * c, :], f32(a_hi[:, c, :]), ALU.subtract).then_inc(lo_ready, 1)
            dve_residual(v, "out2", 0, 2, lambda c: v.wait_ge(block_done, START["out2"] + c + 1), 4, "ffn0")
            dve_diag(v, "ffn0", add=False)
            dve_scale_split(v, "ffn0", "ffn0", DC, lambda c: x[:, c, :], lambda c: gains[:, 1, c:c + 1], lambda c: mod(0, 3, c))
            dve_conv(v, 0)
            dve_split_hidden(v, "down2")
            dve_residual(v, "down2", 0, 5, lambda c: wait_down(v, 1, c), 8, "mix1")
            dve_diag(v, "mix1", add=False)
            dve_scale_split(v, "mix1", "mix1", DC, lambda c: x[:, c, :], lambda c: gains[:, 2, c:c + 1], lambda c: mod(1, 0, c))
            v.wait_ge(wi_landed, 16)
            v.tensor_copy(wi_hi[:].rearrange("p k h -> p (k h)"), wi_raw[:]).then_inc(wi_split, 1)
            v.wait_ge(wi_split, 1)
            v.tensor_tensor(wi_lo[:].rearrange("p k h -> p (k h)"), wi_raw[:], f32(wi_hi[:]).rearrange("p k h -> p (k h)"),
                            ALU.subtract).then_inc(wi_split, 1)
            v.wait_ge(*low_done("mix1", DC - 1))
            v.memset(tmp[64:P, 2, :], 0.0).then_inc(index_init, 1)
            v.memset(tmp[0:64, 3, :], 0.0).then_inc(index_init, 1)
            for i in range(1, TT):
                v.memset(big[:, 20 + i, 0:i * P], 0.0).then_inc(index_init, 1)
                v.tensor_copy(big[:, 20 + i, i * P:(i + 1) * P], causal).then_inc(index_init, 1)
            v.tensor_copy(not_selected[:, 0, 0:P], causal).then_inc(selected, 1)
            v.tensor_scalar(kq_gain[:], vec("dsa_k_norm_2", 0), vec("dsa_q_norm_2", 0), D_LAT ** -0.5, ALU.mult, ALU.mult).then_inc(lat_split, 1)

            def index_add(n):
                i, h = 1 + n // IDX_HEADS, n % IDX_HEADS
                cols = P * (i + 1)
                v.wait_ge(relu_ready, n + 1)
                if n == 0:
                    v.wait_ge(wi_taken, 1)
                    v.wait_ge(index_init, 8)
                else:
                    v.wait_ge(index_added, n)
                v.scalar_tensor_tensor(big[:, 20 + i, 0:cols], probs_t[:, n % 4, 0:cols], wi[:, i, h:h + 1], big[:, 20 + i, 0:cols],
                                       ALU.mult, ALU.add).then_inc(index_added, 1)

            def top_round(n):
                i, turn = 1 + n // (TOPK // 8), n % (TOPK // 8)
                cols = P * (i + 1)
                scores = big[:, 20 + i, 0:cols]
                if turn == 0:
                    v.wait_ge(index_added, i * IDX_HEADS)
                if n:
                    v.wait_ge(top_step, 2 * n)
                v.max(top8[:], scores).then_inc(top_step, 1)
                v.wait_ge(top_step, 2 * n + 1)
                v.match_replace(scores, top8[:], scores, TAKEN).then_inc(top_step, 1)
                if turn == TOPK // 8 - 1:
                    v.wait_ge(top_step, 2 * n + 2)
                    v.tensor_scalar(not_selected[:, i, 0:cols], scores, TAKEN, NEG, ALU.not_equal, ALU.mult).then_inc(selected, 1)

            v.wait_ge(qsum_ready, 1)
            dve_inverse(v, rms, head_sums[:, 0:TT], D_LAT, (qrms_ready, 1), 9)
            dve_write_diag(v).then_inc(k_diag_ready, 1)
            v.wait_ge(lat_split, 2)
            v.wait_ge(*freed("lat", 1))
            v.tensor_tensor(lat_lo[:], k_lat[:], f32(lat_hi[:]), ALU.subtract).then_inc(lat_split, 1)
            v.wait_ge(k_rstd_ready, 1)
            v.scalar_tensor_tensor(k_lat[:], k_lat[:], kq_gain[:, 0:1], rstd_bank[:], ALU.mult, ALU.mult).then_inc(k_scaled, 1)
            for i in range(1, TT):
                for n in range((i - 1) * IDX_HEADS, i * IDX_HEADS):
                    index_add(n)
                    if i > 1:
                        for turn in range(2):
                            top_round((i - 2) * (TOPK // 8) + 2 * (n % IDX_HEADS) + turn)
            for n in range(2 * (TOPK // 8), 3 * (TOPK // 8)):
                top_round(n)
            v.wait_ge(qsum_ready, D_HEADS + 1)
            dve_inverse(v, q_rms, head_sums[:, TT:TT * (D_HEADS + 1)], D_LAT, (qrms_ready, 2), 10)
            v.wait_ge(tables_landed, 32)
            dve_attention(v, d_sems, d_units, lambda h, cols: (y if h < 8 else bias)[:, h % 8, cols - 1::-1], n_stat // 2,
                          low=lambda v, c: dve_low_of_bank(v, "dattn", c, bank[6 + c % 2]),
                          scaled=True)
            dve_residual(v, "out3", 1, 2, lambda c: v.wait_ge(block_done, START["out3"] + c + 1), 4, "ffn1")
            dve_diag(v, "ffn1", add=False)
            dve_scale_split(v, "ffn1", "ffn1", DC, lambda c: x[:, c, :], lambda c: gains[:, 3, c:c + 1], lambda c: mod(1, 3, c))
            dve_conv(v, 1)
            dve_split_hidden(v, "down3")
            dve_residual(v, "down3", 1, 5, lambda c: wait_down(v, 2, c), 8)


def constant_tiles():
    i = np.arange(P)
    row, col = i[:, None], i[None, :]
    tiles = {"ident": row == col, "ones": np.ones((P, P)), "neg_ones": -np.ones((P, P)),
             "neg_suffix": np.where(row >= col, -1.0, 0.0), "upper": col >= row,
             "causal": np.where(col > row, NEG, 0.0), "strict": np.where(row >= col, NEG, 0.0)}
    return np.stack([np.asarray(tiles[n], np.float32) for n in CONSTS], axis=1)


def first_bias():
    p, m = np.arange(P)[:, None], np.arange(S)[None, :]
    dist = p - (m - (S - P))
    count = (dist <= 128) * 1 + (dist % 4 == 0) * 1 + (dist % 16 == 0) * 1
    valid = (dist >= 0) & (count > 0)
    slopes = 2.0 ** (-8.0 * (np.arange(A_HEADS) + 1.0) / A_HEADS)
    b = -slopes[None, :, None] * dist[:, None, :] + np.log(np.maximum(count, 1))[:, None, :]
    return np.where(valid[:, None, :], b, NEG).astype(np.float32)


def bucket_onehot():
    dist = np.maximum(np.arange(SPAN) - (P - 1), 0)
    exact = BUCKETS // 2
    nf = np.maximum(dist, 1).astype(np.float32)
    large = exact + (np.log(nf / np.float32(exact)) / np.float32(math.log(MAX_DIST / exact)) * (BUCKETS - exact)).astype(np.int32)
    bucket = np.where(dist < exact, dist, np.minimum(large, BUCKETS - 1))
    hot = (np.arange(BUCKETS)[:, None] == bucket[None, :]) & (np.arange(SPAN) >= P - 1)[None, :]
    return hot.astype(np.float32)


def tile_blocks(w):
    k, n = w.shape
    return w.reshape(k // P, P, n // P, P).transpose(2, 1, 0, 3).reshape(n // P, P, k)


def token_blocks(w):
    k, n = w.shape
    return w.reshape(k // 256, 2, P, n // S, S).transpose(3, 0, 2, 1, 4).reshape(-1, P, BLOCK)


def chunked(v):
    return v.reshape(-1, P).T


def pair_blocks(w):
    n = w.shape[1] // 2
    return np.stack([tile_blocks(w[:, :n]), tile_blocks(w[:, n:])], axis=1).reshape(-1, P, BLOCK)


def weight_stream(a):
    w_in, sb_in, dsa = a["w_in"][0], a["sb_w_in_2"][0], a["dsa_w_in_2"][0]
    o1 = D_HEADS * D_LAT
    o2 = o1 + D_LAT
    o3 = o2 + IDX_HEADS * IDX_DIM
    o4 = o3 + IDX_DIM
    ki = dsa[:, o3:o4]
    parts = {
        "q": tile_blocks(w_in[:, 0:ATT]), "k": tile_blocks(w_in[:, ATT:2 * ATT]), "v": token_blocks(w_in[:, 2 * ATT:3 * ATT]),
        "u": tile_blocks(w_in[:, 3 * ATT:4 * ATT]), "z": token_blocks(w_in[:, 4 * ATT:5 * ATT]),
        "out1": tile_blocks(a["w_out"][0]), "gu1": pair_blocks(a["w_gate_up"][0]), "down1": a["w_down"][0].reshape(FC, P, D),
        "pe_proj": a["w_pe_proj"][0].reshape(2, P, 2, 4, P).transpose(2, 1, 3, 0, 4).reshape(2, P, BLOCK),
        "pe_gate": tile_blocks(a["w_pe_gate"][0]),
        "bq": tile_blocks(sb_in[:, 0:D]), "bk": tile_blocks(sb_in[:, D:2 * D]), "bv": token_blocks(sb_in[:, 2 * D:3 * D]),
        "out2": tile_blocks(a["sb_w_out_2"][0]),
        "gu2": pair_blocks(a["ffn_w_up_2"][0]), "down2": a["ffn_w_down_2"][0].reshape(FC, P, D),
        "qi": tile_blocks(dsa[:, o2:o3]), "ki": tile_blocks(np.concatenate([ki, ki], axis=1)), "lat": tile_blocks(dsa[:, o1:o2]),
        "dq": tile_blocks(dsa[:, 0:o1]), "uv": a["dsa_w_uv_2"][0].transpose(1, 0, 2).reshape(1, P, BLOCK),
        "out3": tile_blocks(a["dsa_w_out_2"][0]),
        "gu3": pair_blocks(a["ffn_w_up_2"][1]), "down3": a["ffn_w_down_2"][1].reshape(FC, P, D),
    }
    return np.concatenate([parts[name] for name, _ in PHASES], axis=0)


def vectors(a):
    conv_w = a["ffn_conv_w_2"].reshape(2, 3, 2, FC, P)
    conv_b = a["ffn_conv_b_2"].reshape(2, 1, 2, FC, P)
    conv = np.concatenate([conv_w, conv_b], axis=1).transpose(4, 0, 3, 2, 1).reshape(P, -1)
    parts = [conv if name == "conv" else chunked(a[name]) for name, _ in VECS]
    return np.concatenate(parts, axis=1)


def feature_major(t, n):
    return t.reshape(S, n, P).transpose(2, 1, 0)


def kernel(**inputs):
    import concourse.bacc as bacc
    from concourse.bass_utils import run_bass_kernel_spmd

    a = {k: np.asarray(v) for k, v in inputs.items()}
    wi = a["dsa_w_in_2"][0][:, -IDX_HEADS:]
    arrays = {
        "x": feature_major(a["x"][0], DC),
        "p": feature_major(a["p"][0, 0], PLE // P),
        "vecs": vectors(a),
        "stream": weight_stream(a),
        "ada": a["ada_w_2"].reshape(2, D, MOD, P).transpose(0, 2, 3, 1).reshape(2 * MOD, P, D),
        "consts": constant_tiles(),
        "bias": first_bias(),
        "onehot": bucket_onehot(),
        "rel": a["rel_bias_2"],
        "wi": wi.reshape(DC, P, IDX_HEADS).transpose(1, 0, 2).reshape(P, DC * IDX_HEADS),
        "sgu_g": a["sgu_ln_g"][0],
        "sgu_b": a["sgu_ln_b"][0],
        "bs": a["b_spatial"][0].reshape(-1),
        "ws": a["w_spatial"][0].transpose(2, 0, 1),
        "c": a["c_2"][0],
    }
    arrays = {f"in_{k}": np.ascontiguousarray(v) for k, v in arrays.items()}
    nc = bacc.Bacc("TRN2", target_bir_lowering=False, num_devices=1)
    args = [nc.dram_tensor(k, v.shape, F32, kind="ExternalInput").ap() for k, v in arrays.items()]
    scratch = nc.dram_tensor("rel_rows", (D_HEADS, SPAN), F32, kind="Internal").ap()
    out = nc.dram_tensor("out", (P, DC, S), F32, kind="ExternalOutput").ap()
    two_blocks(nc, *args, scratch, out)
    r = run_bass_kernel_spmd(nc, [arrays], core_ids=[0])
    got = r.results[0]["out"]
    return got.transpose(2, 1, 0).reshape(1, S, D)
```
